# Optimizing a Trainium2 kernel written in Bass

```python
import math
import jax, jax.numpy as jnp
from jax import lax
import numpy as np

D_MODEL = 1024
BATCH = 1
SEQ = 512
DEPTH = 2

HEAD_DIM = 64
N_HEADS_DIL = 6
N_HEADS_DSA = 4
N_HEADS_MLA = 6
MIX_WIDTH = (N_HEADS_DIL + N_HEADS_DSA + N_HEADS_MLA) * HEAD_DIM
DILATIONS = ((128, 1), (512, 4), (2048, 16))
IDX_HEADS = 8
IDX_DIM = 64
DSA_TOPK = 256
Q_BLOCK = 128
MLA_Q_RANK = 256
MLA_KV_RANK = 128
MLA_NOPE = 64
MLA_ROPE = 32
MLA_V = 64
ROPE_THETA = 10000.0
N_BUCKETS = 32
MAX_DISTANCE = 2048
N_BIAS_HEADS = N_HEADS_DIL + N_HEADS_DSA
N_EXPERTS = 64
TOP_K = 8
EXPERT_FF = 256
SHARED_FF = 256
ROUTED_SCALE = 2.5
MOE_BLOCK = 128
DN_ALPHA = (2 * DEPTH) ** 0.25
DN_BETA = (8 * DEPTH) ** -0.25
LN_EPS = 1e-5
RMS_EPS = 1e-6

IN_SIZES = (
    N_HEADS_DIL * HEAD_DIM, N_HEADS_DIL * HEAD_DIM, N_HEADS_DIL * HEAD_DIM,
    N_HEADS_DSA * HEAD_DIM, N_HEADS_DSA * HEAD_DIM, N_HEADS_DSA * HEAD_DIM,
    IDX_HEADS * IDX_DIM, IDX_DIM, IDX_HEADS,
    MLA_Q_RANK, MLA_KV_RANK, MLA_ROPE,
)
VALUE_SEGMENTS = (2, 5)
IN_WIDTH = sum(IN_SIZES)

kernel_name = "hybrid_dilated_dsa_mla_moe"

F32 = jnp.float32

def layer_norm(x, g, b):
    xf = x.astype(F32)
    mu = jnp.mean(xf, -1, keepdims=True)
    var = jnp.mean(jnp.square(xf - mu), -1, keepdims=True)
    return ((xf - mu) * lax.rsqrt(var + LN_EPS) * g + b).astype(x.dtype)

def rms_norm(x, g):
    xf = x.astype(F32)
    return (xf * lax.rsqrt(jnp.mean(jnp.square(xf), -1, keepdims=True) + RMS_EPS) * g).astype(x.dtype)

def t5_bucket(dist):
    max_exact = N_BUCKETS // 2
    d_f = jnp.maximum(dist, 1).astype(F32)
    large = max_exact + (jnp.log(d_f / max_exact) / math.log(MAX_DISTANCE / max_exact)
                         * (N_BUCKETS - max_exact)).astype(jnp.int32)
    large = jnp.minimum(large, N_BUCKETS - 1)
    return jnp.where(dist < max_exact, dist, large)

def apply_rope(x, cos, sin):
    half = x.shape[-1] // 2
    x1, x2 = x[..., :half].astype(F32), x[..., half:].astype(F32)
    return jnp.concatenate([x1 * cos - x2 * sin, x2 * cos + x1 * sin], -1).astype(x.dtype)

def split_cols(u):
    out, start = [], 0
    for n in IN_SIZES:
        out.append(u[..., start:start + n])
        start += n
    return out

def dilated_branch(q, k, v, dilation, span, table):
    B, S, H, E = q.shape
    Ls = S // dilation
    nb = -(-Ls // span)
    Lp = nb * span

    def strided(t):
        t = t.reshape(B, Ls, dilation, H, E).transpose(0, 2, 1, 3, 4)
        t = jnp.pad(t, ((0, 0), (0, 0), (0, Lp - Ls), (0, 0), (0, 0)))
        return t.reshape(B, dilation, nb, span, H, E)

    def band(t):
        prev = jnp.pad(t[:, :, :-1], ((0, 0), (0, 0), (1, 0), (0, 0), (0, 0), (0, 0)))
        return jnp.concatenate([prev, t], axis=3)

    qs = strided(q)
    kb, vb = band(strided(k)), band(strided(v))
    qi = jnp.arange(span)[:, None]
    kj = jnp.arange(2 * span)[None, :]
    delta = span + qi - kj
    in_band = (delta >= 0) & (delta <= span)
    has_prev = (jnp.arange(nb)[:, None, None] > 0) | (kj >= span)[None]
    valid = in_band[None] & has_prev
    bias = table[t5_bucket(jnp.maximum(delta, 0) * dilation)].transpose(2, 0, 1)
    logits = jnp.einsum('brnqhe,brnkhe->brnhqk', qs, kb, preferred_element_type=F32) * (HEAD_DIM ** -0.5)
    logits = jnp.where(valid[:, None], logits + bias, -jnp.inf)
    lse = jax.nn.logsumexp(logits, axis=-1)
    p = jnp.exp(logits - lse[..., None])
    o = jnp.einsum('brnhqk,brnkhe->brnqhe', p.astype(v.dtype), vb, preferred_element_type=F32)

    def unstride(t):
        t = t.reshape(B, dilation, Lp, *t.shape[4:])[:, :, :Ls]
        return jnp.swapaxes(t, 1, 2).reshape(B, S, *t.shape[3:])

    return unstride(o), unstride(jnp.swapaxes(lse, 3, 4))

def dilated_mixture(q, k, v, table):
    outs, lses = [], []
    for window, dilation in DILATIONS:
        o, l = dilated_branch(q, k, v, dilation, window // dilation, table)
        outs.append(o)
        lses.append(l)
    wts = jax.nn.softmax(jnp.stack(lses), axis=0)
    return jnp.einsum('gbsh,gbshe->bshe', wts, jnp.stack(outs)).astype(q.dtype)

def dsa_attention(q, k, v, iq, ik, iw, table):
    B, S, H, E = q.shape
    n_sel = min(DSA_TOPK, S // 4)
    nq = S // Q_BLOCK
    key_pos = jnp.arange(S)
    gather = jax.vmap(lambda t, i: t[i])

    def to_blocks(t):
        return jnp.swapaxes(t.reshape(B, nq, Q_BLOCK, *t.shape[2:]), 0, 1)

    def block(args):
        qb, iqb, iwb, start = args
        t = start + jnp.arange(Q_BLOCK)
        causal = key_pos[None, :] <= t[:, None]
        rel = jax.nn.relu(jnp.einsum('bqhe,bse->bqhs', iqb, ik, preferred_element_type=F32))
        score = jnp.einsum('bqh,bqhs->bqs', iwb.astype(F32), rel)
        score = jnp.where(causal[None], score, -jnp.inf)
        _, idx = lax.top_k(score, n_sel)
        valid = idx <= t[None, :, None]
        ksel, vsel = gather(k, idx), gather(v, idx)
        bias = table[t5_bucket(jnp.maximum(t[None, :, None] - idx, 0))]
        logits = jnp.einsum('bqhe,bqkhe->bqhk', qb, ksel, preferred_element_type=F32) * (HEAD_DIM ** -0.5)
        logits = jnp.where(valid[:, :, None, :], logits + jnp.swapaxes(bias, 2, 3), -jnp.inf)
        p = jax.nn.softmax(logits, axis=-1)
        return jnp.einsum('bqhk,bqkhe->bqhe', p.astype(v.dtype), vsel, preferred_element_type=F32)

    out = lax.map(block, (to_blocks(q), to_blocks(iq), to_blocks(iw), jnp.arange(nq) * Q_BLOCK))
    return jnp.swapaxes(out, 0, 1).reshape(B, S, H, E).astype(q.dtype)

def mla_attention(cq, ckv, k_rope, positions, q_norm, w_uq, kv_norm, w_ukv):
    B, S, _ = cq.shape
    q = (rms_norm(cq, q_norm) @ w_uq).reshape(B, S, N_HEADS_MLA, MLA_NOPE + MLA_ROPE)
    kv = (rms_norm(ckv, kv_norm) @ w_ukv).reshape(B, S, N_HEADS_MLA, MLA_NOPE + MLA_V)
    inv = ROPE_THETA ** (-jnp.arange(0, MLA_ROPE, 2, dtype=F32) / MLA_ROPE)
    ang = positions.astype(F32)[..., None] * inv
    cos, sin = jnp.cos(ang), jnp.sin(ang)
    q_nope = q[..., :MLA_NOPE]
    q_rope = apply_rope(q[..., MLA_NOPE:], cos[:, :, None], sin[:, :, None])
    k_nope, v = kv[..., :MLA_NOPE], kv[..., MLA_NOPE:]
    k_r = apply_rope(k_rope, cos, sin)
    scale = (MLA_NOPE + MLA_ROPE) ** -0.5
    nq = S // Q_BLOCK
    key_pos = jnp.arange(S)

    def to_blocks(t):
        return jnp.swapaxes(t.reshape(B, nq, Q_BLOCK, *t.shape[2:]), 0, 1)

    def block(args):
        qn, qr, start = args
        t = start + jnp.arange(Q_BLOCK)
        logits = (jnp.einsum('bqhe,bshe->bhqs', qn, k_nope, preferred_element_type=F32)
                  + jnp.einsum('bqhe,bse->bhqs', qr, k_r, preferred_element_type=F32)) * scale
        logits = jnp.where(key_pos[None, :] <= t[:, None], logits, -jnp.inf)
        p = jax.nn.softmax(logits, axis=-1)
        return jnp.einsum('bhqs,bshe->bqhe', p.astype(v.dtype), v, preferred_element_type=F32)

    out = lax.map(block, (to_blocks(q_nope), to_blocks(q_rope), jnp.arange(nq) * Q_BLOCK))
    return jnp.swapaxes(out, 0, 1).reshape(B, S, N_HEADS_MLA, MLA_V).astype(cq.dtype)

def hybrid_mixer(x, positions, w_in, q_norm, w_uq, kv_norm, w_ukv, w_out, rel_bias):
    B, S, _ = x.shape
    dq, dk, dv, sq, sk, sv, iq, ik, iw, cq, ckv, kr = split_cols(x @ w_in)
    heads = lambda t, h: t.reshape(B, S, h, -1)
    o_a = dilated_mixture(heads(dq, N_HEADS_DIL), heads(dk, N_HEADS_DIL), heads(dv, N_HEADS_DIL),
                          rel_bias[:, :N_HEADS_DIL])
    o_b = dsa_attention(heads(sq, N_HEADS_DSA), heads(sk, N_HEADS_DSA), heads(sv, N_HEADS_DSA),
                        heads(iq, IDX_HEADS), ik, iw, rel_bias[:, N_HEADS_DIL:])
    o_c = mla_attention(cq, ckv, kr, positions, q_norm, w_uq, kv_norm, w_ukv)
    o = jnp.concatenate([o_a.reshape(B, S, -1), o_b.reshape(B, S, -1), o_c.reshape(B, S, -1)], -1)
    return o.astype(x.dtype) @ w_out

def moe_ffn(x, router_w, router_bias, w1, w3, w2, sw1, sw3, sw2):
    B, S, D = x.shape
    xf = x.reshape(-1, D)
    T = xf.shape[0]
    scores = jax.nn.sigmoid(jnp.matmul(xf, router_w, preferred_element_type=F32))
    _, idx = lax.top_k(scores + router_bias.astype(F32), TOP_K)
    gates = jnp.take_along_axis(scores, idx, -1)
    gates = gates / jnp.sum(gates, -1, keepdims=True) * ROUTED_SCALE
    n_assign = T * TOP_K
    e_flat = idx.reshape(-1)
    tok_flat = jnp.repeat(jnp.arange(T, dtype=jnp.int32), TOP_K)
    g_flat = gates.reshape(-1)
    order = jnp.argsort(e_flat)
    e_s, tok_s, g_s = e_flat[order], tok_flat[order], g_flat[order]
    counts = jnp.bincount(e_flat, length=N_EXPERTS)
    starts = jnp.cumsum(counts) - counts
    pcounts = (counts + MOE_BLOCK - 1) // MOE_BLOCK * MOE_BLOCK
    pstarts = jnp.cumsum(pcounts) - pcounts
    dest = pstarts[e_s] + (jnp.arange(n_assign) - starts[e_s])
    n_blocks = -(-n_assign // MOE_BLOCK) + N_EXPERTS
    n_rows = n_blocks * MOE_BLOCK
    row_tok = jnp.zeros((n_rows,), jnp.int32).at[dest].set(tok_s)
    row_gate = jnp.zeros((n_rows,), F32).at[dest].set(g_s)
    block_end = jnp.cumsum(pcounts) // MOE_BLOCK
    block_expert = jnp.minimum(jnp.searchsorted(block_end, jnp.arange(n_blocks), side='right'), N_EXPERTS - 1)

    def expert_block(args):
        tok, gate, e = args
        h = xf[tok]
        y = (jax.nn.silu(h @ w1[e]) * (h @ w3[e])) @ w2[e]
        return y.astype(F32) * gate[:, None]

    ys = lax.map(expert_block, (row_tok.reshape(n_blocks, MOE_BLOCK), row_gate.reshape(n_blocks, MOE_BLOCK),
                                block_expert))
    routed = jnp.zeros((T, D), F32).at[row_tok].add(ys.reshape(n_rows, D))
    shared = (jax.nn.silu(xf @ sw1) * (xf @ sw3)) @ sw2
    return (routed + shared.astype(F32)).astype(x.dtype).reshape(B, S, D)

def setup_inputs(seed: int = 0) -> dict:
    key = jax.random.key(seed)
    ks = jax.random.split(key, 24)
    nrm = lambda k, s: jax.random.normal(k, s, F32)
    col_scale = jnp.concatenate([jnp.full((n,), DN_BETA if i in VALUE_SEGMENTS else 1.0, F32)
                                 for i, n in enumerate(IN_SIZES)])
    ukv_scale = jnp.tile(jnp.concatenate([jnp.ones((MLA_NOPE,), F32), jnp.full((MLA_V,), DN_BETA, F32)]),
                         N_HEADS_MLA)
    return {
        "x": nrm(ks[0], (BATCH, SEQ, D_MODEL)),
        "positions": jnp.broadcast_to(jnp.arange(SEQ, dtype=jnp.int32), (BATCH, SEQ)),
        "w_in": nrm(ks[1], (DEPTH, D_MODEL, IN_WIDTH)) * D_MODEL ** -0.5 * col_scale,
        "mla_q_norm": 1.0 + 0.02 * nrm(ks[2], (DEPTH, MLA_Q_RANK)),
        "mla_w_uq": nrm(ks[3], (DEPTH, MLA_Q_RANK, N_HEADS_MLA * (MLA_NOPE + MLA_ROPE))) * MLA_Q_RANK ** -0.5,
        "mla_kv_norm": 1.0 + 0.02 * nrm(ks[4], (DEPTH, MLA_KV_RANK)),
        "mla_w_ukv": nrm(ks[5], (DEPTH, MLA_KV_RANK, N_HEADS_MLA * (MLA_NOPE + MLA_V))) * MLA_KV_RANK ** -0.5 * ukv_scale,
        "w_out": nrm(ks[6], (DEPTH, MIX_WIDTH, D_MODEL)) * MIX_WIDTH ** -0.5 * DN_BETA,
        "ln1_g": 1.0 + 0.02 * nrm(ks[7], (DEPTH, D_MODEL)),
        "ln1_b": 0.02 * nrm(ks[8], (DEPTH, D_MODEL)),
        "router_w": nrm(ks[9], (DEPTH, D_MODEL, N_EXPERTS)) * D_MODEL ** -0.5,
        "router_bias": 0.01 * nrm(ks[10], (DEPTH, N_EXPERTS)),
        "exp_w1": nrm(ks[11], (DEPTH, N_EXPERTS, D_MODEL, EXPERT_FF)) * D_MODEL ** -0.5,
        "exp_w3": nrm(ks[12], (DEPTH, N_EXPERTS, D_MODEL, EXPERT_FF)) * D_MODEL ** -0.5,
        "exp_w2": nrm(ks[13], (DEPTH, N_EXPERTS, EXPERT_FF, D_MODEL)) * EXPERT_FF ** -0.5 * DN_BETA,
        "sh_w1": nrm(ks[14], (DEPTH, D_MODEL, SHARED_FF)) * D_MODEL ** -0.5,
        "sh_w3": nrm(ks[15], (DEPTH, D_MODEL, SHARED_FF)) * D_MODEL ** -0.5,
        "sh_w2": nrm(ks[16], (DEPTH, SHARED_FF, D_MODEL)) * SHARED_FF ** -0.5 * DN_BETA,
        "ln2_g": 1.0 + 0.02 * nrm(ks[17], (DEPTH, D_MODEL)),
        "ln2_b": 0.02 * nrm(ks[18], (DEPTH, D_MODEL)),
        "rel_bias": 0.3 * nrm(ks[19], (N_BUCKETS, N_BIAS_HEADS)),
    }

def reference(x, positions, w_in, mla_q_norm, mla_w_uq, mla_kv_norm, mla_w_ukv, w_out, ln1_g, ln1_b,
              router_w, router_bias, exp_w1, exp_w3, exp_w2, sh_w1, sh_w3, sh_w2, ln2_g, ln2_b, rel_bias):
    for l in range(DEPTH):
        mix = hybrid_mixer(x, positions, w_in[l], mla_q_norm[l], mla_w_uq[l], mla_kv_norm[l], mla_w_ukv[l],
                           w_out[l], rel_bias)
        x = layer_norm(DN_ALPHA * x + mix, ln1_g[l], ln1_b[l])
        ffn = moe_ffn(x, router_w[l], router_bias[l], exp_w1[l], exp_w3[l], exp_w2[l],
                      sh_w1[l], sh_w3[l], sh_w2[l])
        x = layer_norm(DN_ALPHA * x + ffn, ln2_g[l], ln2_b[l])
    return x


_drawn_inputs = setup_inputs


def setup_inputs(seed=0):
    import zlib

    import numpy as np

    out = dict(_drawn_inputs(seed))
    spreads = {}
    factors = {'mla_q_norm': 8.0, 'mla_kv_norm': 7.538}
    for name, (base, spread) in spreads.items():
        noise = np.random.default_rng([zlib.crc32(name.encode()), seed]).standard_normal(out[name].shape)
        drawn = base * np.exp(spread * noise) if base else spread * noise
        out[name] = __import__('jax').numpy.asarray(drawn.astype(out[name].dtype))
    for name, factor in factors.items():
        out[name] = (out[name] * factor).astype(out[name].dtype)
    return out
```

```python
import math
from contextlib import ExitStack

import numpy as np

import concourse.bass as bass
import concourse.mybir as mybir
from concourse.alu_op_type import AluOpType as ALU

F32 = mybir.dt.float32
I32 = mybir.dt.int32
BF16 = mybir.dt.bfloat16
ACT = mybir.ActivationFunctionType
AX = mybir.AxisListType

P = 128
D, SEQ, DEPTH = 1024, 512, 2
NT = SEQ // P
KD = D // P
HD = 64
H_DIL, H_DSA, H_MLA = 6, 4, 6
DILATIONS = ((128, 1), (512, 4), (2048, 16))
H_IDX = 8
TOPK_KEYS = min(256, SEQ // 4)
RQ, RKV, NOPE, ROPE = 256, 128, 64, 32
MQ = NOPE + ROPE
N_BUCKETS, MAX_DISTANCE = 32, 2048
NE, TOPK, FF, SFF = 64, 8, 256, 256
ROUTED_SCALE = 2.5
ALPHA = (2 * DEPTH) ** 0.25
LN_EPS, RMS_EPS = 1e-5, 1e-6
SCALE = HD ** -0.5
MLA_SCALE = MQ ** -0.5
NEG = -1e30
TAKEN = -3e38
CAP = 104
MAX_PASSES = -(-SEQ // CAP)
ACC_ROWS = SEQ + P
NOT_ROUTED = 4096.0

C_DQ, C_DK, C_DV = 0, 384, 768
C_SQ, C_SK, C_SV = 1152, 1408, 1664
C_IQ, C_IK, C_IW = 1920, 2432, 2496
C_CQ, C_CKV, C_KR = 2504, 2760, 2888
IN_WIDTH = 2920
CHUNKS = ((C_IW, 264), (C_CKV, 160), (C_IQ, 256), (C_IQ + 256, 256),
          (0, 256), (256, 256), (512, 256), (C_DV, 192), (C_DV + 192, 192),
          (C_SQ, 256), (C_SK, 256), (C_SV, 256))
CHUNK_MAX = 264
W_SLOTS = 3
REST0 = C_IW
PEN_AT = {1: 0, 2: 2 * P, 3: 5 * P}
PEN_COLUMNS = 9 * P
SPAN = P + SEQ - 1


def _buckets(distance):
    exact = N_BUCKETS // 2
    d = np.maximum(distance, 1).astype(np.float64)
    large = exact + (np.log(d / exact) / math.log(MAX_DISTANCE / exact) * (N_BUCKETS - exact)).astype(np.int64)
    return np.where(distance < exact, distance, np.minimum(large, N_BUCKETS - 1))


def _constants():
    k = np.arange(SPAN + 1)
    dist = SEQ - 1 - k
    causal = dist >= 0
    onehot = ((_buckets(np.maximum(dist, 0))[None, :] == np.arange(N_BUCKETS)[:, None]) & causal)
    count = sum(((dist % d == 0) & (dist <= w)).astype(np.int64) for w, d in DILATIONS)
    logcount = np.where(causal & (count > 0), np.log(np.maximum(count, 1)), NEG)
    addend = np.concatenate([np.repeat(logcount[None], H_DIL, 0),
                             np.repeat(np.where(causal, 0.0, NEG)[None], H_DSA, 0)])
    p = np.arange(P)
    inv = 10000.0 ** (-np.arange(0, ROPE, 2) / ROPE)
    square = np.concatenate([np.eye(P), p[:, None] < p[None, :], np.ones((P, P))], 1)
    once = np.concatenate([np.eye(P)[::-1], np.repeat(np.arange(CAP)[None], P, 0)], 1)
    row = np.concatenate([np.repeat(inv[None], P, 0), (SEQ + p)[:, None],
                          p[:, None] + P * np.arange(NT)[None] - SEQ], 1)
    mask = np.where(p[:, None] + (SEQ - P) - np.arange(SEQ)[None] >= 0, 0.0, NEG)
    f = np.float32
    return {
        "c_square": square.astype(f),
        "c_once": once.astype(f),
        "c_row": row.astype(f),
        "c_mask": mask.astype(f),
        "c_onehot": onehot.astype(f),
        "c_addend": (addend / SCALE).astype(f),
    }


def _named(ctx, nc, names):
    return {n: ctx.enter_context(nc.semaphore(n)) for n in names.split()}


def _restart(nc, sems):
    numbers = [s.num for s in sems.values()]
    span = range(min(numbers), max(numbers) + 1)
    nc.gpsimd.dma_reset(span)
    nc.gpsimd.sem_clear(span)
    nc.all_engine_barrier()


def _setup(nc, d, sb):
    with ExitStack() as ctx:
        S = _named(ctx, nc, "consts_in x_in table_in positions_in bias_psum bias_row bias_row_out bias_in bias_turned bias_out "
                            "angle quarter sines zeros zeros_out numbers")
        raw = ctx.enter_context(nc.sbuf_tensor("raw_table", [N_BUCKETS, 10], F32))
        onehot = ctx.enter_context(nc.sbuf_tensor("onehot", [N_BUCKETS, SPAN + 1], F32))
        addend = ctx.enter_context(nc.sbuf_tensor("addend", [10, SPAN + 1], F32))
        brow = ctx.enter_context(nc.sbuf_tensor("brow", [10, SPAN + 1], F32))
        pos_i = ctx.enter_context(nc.sbuf_tensor("pos_i", [P, NT], I32))
        pos_f = ctx.enter_context(nc.sbuf_tensor("pos_f", [P, NT], F32))
        ang = ctx.enter_context(nc.sbuf_tensor("ang", [P, NT, 2, ROPE // 2], F32))
        turns = ctx.enter_context(nc.sbuf_tensor("turns", [P, NT, ROPE // 2], F32))
        turns_i = ctx.enter_context(nc.sbuf_tensor("turns_i", [P, NT, ROPE // 2], I32))
        zero = ctx.enter_context(nc.sbuf_tensor("zero", [P, D], F32))
        once = ctx.enter_context(nc.sbuf_tensor("once", [P, P + CAP], F32))
        flipped = ctx.enter_context(nc.sbuf_tensor("flipped", [P, 10, SEQ], F32))
        ps = ctx.enter_context(nc.psum_tensor("ps_bias", [P, 2, 512], F32))
        ps_f = [ctx.enter_context(nc.psum_tensor(f"ps_flip{i}", [P, 512], F32)) for i in range(4)]
        half = (SPAN + 1) // 2
        with nc.Block() as block:
            @block.sync
            def _(sp):
                sp.dma_start(raw[:], d["rel_bias"]).then_inc(S["table_in"], 16)
                sp.dma_start(onehot[:], d["c_onehot"]).then_inc(S["table_in"], 16)
                sp.dma_start(addend[:], d["c_addend"]).then_inc(S["table_in"], 16)
                sp.dma_start(pos_i[:], d["positions"].rearrange("o (t p) -> p (o t)", p=P), allow_slow_non_contiguous=True).then_inc(S["positions_in"], 16)
                sp.dma_start(sb["row"][:], d["c_row"]).then_inc(S["positions_in"], 16)
                sp.dma_start(sb["square"][:], d["c_square"]).then_inc(S["consts_in"], 16)
                sp.dma_start(sb["mask"][:], d["c_mask"]).then_inc(S["consts_in"], 16)
                sp.dma_start(once[:], d["c_once"]).then_inc(S["consts_in"], 16)
                sp.dma_start(sb["x"][:], d["x"].rearrange("o (t p) m -> p (o t) m", p=P)).then_inc(S["x_in"], 16)
                sp.wait_ge(S["zeros"], 1)
                sp.dma_start(d["x1_rows"][SEQ:ACC_ROWS, :], zero[:]).then_inc(S["zeros_out"], 16)
                sp.dma_start(d["acc_rows"][SEQ:ACC_ROWS, :], zero[:]).then_inc(S["zeros_out"], 16)
                sp.wait_ge(S["bias_row"], 2)
                sp.dma_start(d["bias_rows"], brow[:]).then_inc(S["bias_row_out"], 16)
                sp.wait_ge(S["bias_row_out"], 16)
                sp.dma_start(flipped[:], bass.AP(d["bias_rows"].tensor, 0, [[1, P], [SPAN + 1, 10], [1, SEQ]])
                             ).then_inc(S["bias_in"], 16)
                sp.wait_ge(S["zeros_out"], 32)
                sp.wait_ge(S["consts_in"], 48)
                sp.wait_ge(S["x_in"], 16)

            @block.tensor
            def _(pe):
                pe.wait_ge(S["table_in"], 48)
                for c in range(2):
                    pe.matmul(ps[0:10, c, 0:half], raw[:], onehot[:, c * half:(c + 1) * half],
                              start=True, stop=True).then_inc(S["bias_psum"], 1)
                pe.wait_ge(S["consts_in"], 48)
                pe.wait_ge(S["bias_in"], 16)
                for h in range(10):
                    if h >= 4:
                        pe.wait_ge(S["bias_out"], h - 3)
                    pe.matmul(ps_f[h % 4][:], once[:, 0:P], flipped[:, h, :], start=True, stop=True
                              ).then_inc(S["bias_turned"], 1)

            @block.vector
            def _(dve):
                dve.memset(zero[:], 0.0).then_inc(S["zeros"], 1)
                dve.wait_ge(S["consts_in"], 48)
                dve.tensor_copy(sb["number"][:], once[:, P:P + CAP]).then_inc(S["numbers"], 1)
                dve.wait_ge(S["positions_in"], 32)
                dve.tensor_copy(pos_f[:], pos_i[:]).then_inc(S["angle"], 1)
                dve.wait_ge(S["angle"], 1)
                for t in range(NT):
                    dve.tensor_scalar(ang[:, t, 1, :], sb["row"][:, 0:ROPE // 2], pos_f[:, t:t + 1], None,
                                      ALU.mult).then_inc(S["angle"], 1)
                sines = ang[:, :, 1, :]
                steps = 1 + NT

                def done(i):
                    nonlocal steps
                    i.then_inc(S["angle"], 1)
                    steps += 1
                    dve.wait_ge(S["angle"], steps)

                dve.wait_ge(S["angle"], steps)
                done(dve.tensor_scalar(turns[:], sines, 1.0 / (2 * math.pi), None, ALU.mult))
                done(dve.tensor_copy(turns_i[:], turns[:]))
                done(dve.tensor_copy(turns[:], turns_i[:]))
                c1 = 6.28125
                c2 = float(np.float32(round((2 * math.pi - c1) * 2 ** 21) / 2 ** 21))
                c3 = 2 * math.pi - c1 - c2
                for part in (c1, c2, c3):
                    done(dve.scalar_tensor_tensor(out=sines, in0=turns[:], scalar=-part, in1=sines,
                                                  op0=ALU.mult, op1=ALU.add))
                done(dve.tensor_scalar(ang[:, :, 0, :], sines, math.pi / 2, None, ALU.add))
                done(dve.tensor_scalar(turns[:], ang[:, :, 0, :], math.pi, -2 * math.pi, ALU.is_gt, ALU.mult))
                done(dve.tensor_tensor(ang[:, :, 0, :], ang[:, :, 0, :], turns[:], ALU.add))
                lim = 3.1415925
                dve.tensor_scalar(ang[:], ang[:], lim, -lim, ALU.min, ALU.max).then_inc(S["quarter"], 1)
                for c in range(2):
                    dve.wait_ge(S["bias_psum"], c + 1)
                    dve.scalar_tensor_tensor(out=brow[:, c * half:(c + 1) * half], in0=ps[0:10, c, 0:half],
                                             scalar=1.0 / SCALE, in1=addend[:, c * half:(c + 1) * half],
                                             op0=ALU.mult, op1=ALU.add).then_inc(S["bias_row"], 1)

            @block.scalar
            def _(act):
                act.wait_ge(S["quarter"], 1)
                act.activation(sb["rope"][:], ang[:], ACT.Sin).then_inc(S["sines"], 1)
                for h in range(10):
                    act.wait_ge(S["bias_turned"], h + 1)
                    act.copy(sb["bias"][:, h, :], ps_f[h % 4][:]).then_inc(S["bias_out"], 1)
        _restart(nc, S)


def _units():
    u = [("xT", k) for k in range(KD)]
    u += [("rest", 0, t) for t in range(NT)] + [("rest", 1, t) for t in range(NT)]
    u += [("ik",)] + [("iq", m) for m in range(4)]
    u += [("cqT", j) for j in range(2)] + [("ckvT",)]
    u += [("idx", i, g) for i in (3, 2, 1) for g in range(H_IDX)]
    u += [("mq", t, c) for t in range(NT) for c in range(2)]
    u += [("dqk", m) for m in range(6)]
    u += [("kn", h) for h in range(H_MLA)] + [("mv", t) for t in range(NT)]
    u += [("qT", h) for h in range(H_MLA)] + [("krT",)]
    u += [("dv", c, t) for c in range(2) for t in range(NT)]
    u += [("sqk", m) for m in range(4)] + [("sv", t) for t in range(NT)]
    return u


BANKS1 = 8


def _projections(nc, d, sb, l):
    units = _units()
    place = {x: i for i, x in enumerate(units)}
    chunk_of = {"rest": lambda x: x[1], "iq": lambda x: 2 + x[1] // 2, "dqk": lambda x: 4 + x[1] // 2,
                "dv": lambda x: 7 + x[1], "sqk": lambda x: 9 + x[1] // 2, "sv": lambda x: 11}
    last_use = {chunk_of[x[0]](x): u for u, x in enumerate(units) if x[0] in chunk_of}
    with ExitStack() as ctx:
        S = _named(ctx, nc, "w0_in w1_in w2_in ik_w_in small_in unit_made unit_out rel_used "
                            "squares mean_squares root latent_ready dve_step q_roped k_roped pool_step kr_zero")
        w_in_sem = [S[f"w{i}_in"] for i in range(W_SLOTS)]
        wbuf = ctx.enter_context(nc.sbuf_tensor("wbuf", [P, W_SLOTS, KD, CHUNK_MAX], F32))
        w_ik = ctx.enter_context(nc.sbuf_tensor("w_ik", [P, KD, 2, HD], F32))
        w_uq = ctx.enter_context(nc.sbuf_tensor("w_uq", [P, 2, H_MLA * MQ], F32))
        w_ukv = ctx.enter_context(nc.sbuf_tensor("w_ukv", [P, H_MLA, 2, HD], F32))
        g_q = ctx.enter_context(nc.sbuf_tensor("g_q", [P, 2], F32))
        g_kv = ctx.enter_context(nc.sbuf_tensor("g_kv", [P, 1], F32))
        iqT = ctx.enter_context(nc.sbuf_tensor("iqT", [P, 4, SEQ], F32))
        ikT = ctx.enter_context(nc.sbuf_tensor("ikT", [P, SEQ], F32))
        rest = ctx.enter_context(nc.sbuf_tensor("rest", [P, NT, IN_WIDTH - REST0], F32))
        cqT = ctx.enter_context(nc.sbuf_tensor("cqT", [P, 2, SEQ], F32))
        ckvT = ctx.enter_context(nc.sbuf_tensor("ckvT", [P, SEQ], F32))
        q_tm = ctx.enter_context(nc.sbuf_tensor("q_tm", [P, NT, H_MLA, MQ], F32))
        rot = ctx.enter_context(nc.sbuf_tensor("rot", [P, 2, NT, H_MLA, ROPE // 2], F32))
        kr = ctx.enter_context(nc.sbuf_tensor("kr", [P, NT, MQ], F32))
        rel = ctx.enter_context(nc.sbuf_tensor("rel", [P, 2, SEQ], F32))
        score = ctx.enter_context(nc.sbuf_tensor("score", [P, PEN_COLUMNS], F32))
        top8 = ctx.enter_context(nc.sbuf_tensor("top8", [P, 8], F32))
        ms = ctx.enter_context(nc.sbuf_tensor("ms", [P, 2, NT], F32))
        ps = [ctx.enter_context(nc.psum_tensor(f"pp{i}", [P, 512], F32)) for i in range(BANKS1)]
        xT, x_sb = sb["xT"], sb["x"]
        junk = score
        ident = sb["square"][:, 0:P]
        iw = lambda i, g: rest[:, i, g:g + 1]
        cq = rest[:, :, C_CQ - REST0:C_CKV - REST0]
        ckv = rest[:, :, C_CKV - REST0:C_KR - REST0]
        kraw = rest[:, :, C_KR - REST0:IN_WIDTH - REST0]
        cos, sin = sb["rope"][:, :, 0, :], sb["rope"][:, :, 1, :]

        with nc.Block() as block:
            @block.sync
            def _(sp):
                w = d["w_in"][bass.ds(l, 1)].rearrange("o (p k) c -> p (o k) c", k=KD)

                def chunk(c):
                    if c >= W_SLOTS:
                        sp.wait_ge(S["unit_made"], last_use[c - W_SLOTS] + 1)
                    c0, n = CHUNKS[c]
                    sp.dma_start(wbuf[:, c % W_SLOTS, :, 0:n], w[:, :, c0:c0 + n]).then_inc(w_in_sem[c % W_SLOTS], 16)

                chunk(0)
                chunk(1)
                for j in range(2):
                    sp.dma_start(w_ik[:, :, j, :], w[:, :, C_IK:C_IK + HD]).then_inc(S["ik_w_in"], 16)
                sp.dma_start(g_q[:], d["mla_q_norm"][bass.ds(l, 1)].rearrange("o (j p) -> p (o j)", p=P), allow_slow_non_contiguous=True).then_inc(S["small_in"], 16)
                sp.dma_start(g_kv[:], d["mla_kv_norm"][bass.ds(l, 1)].rearrange("o (j p) -> p (o j)", p=P), allow_slow_non_contiguous=True).then_inc(S["small_in"], 16)
                sp.dma_start(w_uq[:], d["mla_w_uq"][bass.ds(l, 1)].rearrange("o (j p) c -> p (o j) c", p=P)).then_inc(S["small_in"], 16)
                sp.dma_start(w_ukv[:].rearrange("p h a c -> p (h a c)"),
                             d["mla_w_ukv"][bass.ds(l, 1)].rearrange("o p c -> p (o c)")).then_inc(S["small_in"], 16)
                for c in range(2, len(CHUNKS)):
                    chunk(c)

            @block.tensor
            def _(pe):
                waited = set()
                for u, x in enumerate(units):
                    kind = x[0]
                    out = ps[u % BANKS1]
                    if u >= BANKS1:
                        pe.wait_ge(S["unit_out"], u - BANKS1 + 1)
                    if kind in chunk_of and chunk_of[kind](x) not in waited:
                        c = chunk_of[kind](x)
                        waited.add(c)
                        pe.wait_ge(w_in_sem[c % W_SLOTS], 16 * (c // W_SLOTS + 1))
                        wc = wbuf[:, c % W_SLOTS]
                    if x == ("rest", 0, 0):
                        pe.wait_ge(S["unit_out"], KD)
                    if kind == "xT":
                        for t in range(NT):
                            mm = pe.transpose(out[:, t * P:(t + 1) * P], x_sb[:, t, x[1]::KD], ident)
                    elif kind in ("rest", "dv", "sv"):
                        t = x[-1]
                        n = CHUNKS[c][1]
                        for k in range(KD):
                            mm = pe.matmul(out[:, 0:n], xT[:, k, t * P:(t + 1) * P], wc[:, k, 0:n],
                                           start=(k == 0), stop=(k == KD - 1))
                    elif kind in ("iq", "dqk", "sqk"):
                        m = x[1] % 2
                        for k in range(KD):
                            mm = pe.matmul(out[:, :], wc[:, k, m * P:(m + 1) * P], xT[:, k, :],
                                           start=(k == 0), stop=(k == KD - 1))
                    elif kind == "ik":
                        pe.wait_ge(S["ik_w_in"], 32)
                        for k in range(KD):
                            mm = pe.matmul(out[:, :], w_ik[:, k].rearrange("p a c -> p (a c)"), xT[:, k, :],
                                           start=(k == 0), stop=(k == KD - 1))
                    elif kind in ("cqT", "ckvT"):
                        if x == ("cqT", 0):
                            pe.wait_ge(S["latent_ready"], 2 * NT)
                        for t in range(NT):
                            src = cq[:, t, x[1] * P:(x[1] + 1) * P] if kind == "cqT" else ckv[:, t, :]
                            mm = pe.transpose(out[:, t * P:(t + 1) * P], src, ident)
                    elif kind == "idx":
                        i, g = x[1:]
                        if x == ("idx", 3, 0):
                            pe.wait_ge(S["unit_out"], place[("iq", 3)] + 1)
                        a = HD * (g % 2)
                        mm = pe.matmul(out[:, 0:P * (i + 1)], iqT[a:a + HD, g // 2, i * P:(i + 1) * P],
                                       ikT[a:a + HD, 0:P * (i + 1)], start=True, stop=True)
                    elif kind == "mq":
                        t, c2 = x[1:]
                        if x == ("mq", 0, 0):
                            pe.wait_ge(S["unit_out"], place[("ckvT",)] + 1)
                            pe.wait_ge(S["small_in"], 64)
                        n = H_MLA * MQ // 2
                        for j in range(2):
                            mm = pe.matmul(out[:, 0:n], cqT[:, j, t * P:(t + 1) * P],
                                           w_uq[:, j, c2 * n:(c2 + 1) * n], start=(j == 0), stop=(j == 1))
                    elif kind == "kn":
                        mm = pe.matmul(out[0:HD, :], w_ukv[:, x[1], 0, :], ckvT[:, :], start=True, stop=True)
                    elif kind == "mv":
                        mm = pe.matmul(out[:, 0:H_MLA * HD].rearrange("p (h c) -> p h c", c=HD),
                                       ckvT[:, x[1] * P:(x[1] + 1) * P], w_ukv[:, :, 1, :],
                                       start=True, stop=True)
                    elif kind == "qT":
                        if x[1] == 0:
                            pe.wait_ge(S["q_roped"], 2)
                        for t in range(NT):
                            mm = pe.transpose(out[0:MQ, t * P:(t + 1) * P], q_tm[:, t, x[1], :], ident)
                    elif kind == "krT":
                        pe.wait_ge(S["k_roped"], 2)
                        pe.wait_ge(S["kr_zero"], 1)
                        for t in range(NT):
                            mm = pe.transpose(out[0:MQ, t * P:(t + 1) * P], kr[:, t, :], ident)
                    mm.then_inc(S["unit_made"], 1)

            @block.scalar
            def _(act):
                for u, x in enumerate(units):
                    kind = x[0]
                    src = ps[u % BANKS1]
                    act.wait_ge(S["unit_made"], u + 1)
                    if kind == "xT":
                        o = act.copy(xT[:, x[1], :], src[:, :])
                    elif kind == "rest":
                        c0, n = CHUNKS[x[1]]
                        o = act.copy(rest[:, x[2], c0 - REST0:c0 - REST0 + n], src[:, 0:n])
                    elif kind == "ik":
                        o = act.copy(ikT[:, :], src[:, :])
                    elif kind == "iq":
                        o = act.copy(iqT[:, x[1], :], src[:, :])
                    elif kind == "cqT":
                        if x[1] == 0:
                            act.wait_ge(S["small_in"], 64)
                        o = act.activation(cqT[:, x[1], :], src[:, :], ACT.Copy, scale=g_q[:, x[1]:x[1] + 1])
                    elif kind == "ckvT":
                        o = act.activation(ckvT[:, :], src[:, :], ACT.Copy, scale=g_kv[:, 0:1])
                    elif kind == "idx":
                        n = u - place[("idx", 3, 0)]
                        if n >= 2:
                            act.wait_ge(S["rel_used"], n - 1)
                        w = P * (x[1] + 1)
                        o = act.activation(rel[:, n % 2, 0:w], src[:, 0:w], ACT.Relu)
                    elif kind == "mq":
                        hh = H_MLA // 2
                        o = act.copy(q_tm[:, x[1], x[2] * hh:(x[2] + 1) * hh, :].rearrange("p h c -> p (h c)"),
                                     src[:, 0:hh * MQ])
                    elif kind == "kn":
                        o = act.copy(sb["mkT"][0:HD, x[1], :], src[0:HD, :])
                    elif kind == "mv":
                        o = act.copy(sb["mv"][:, x[1], :], src[:, 0:H_MLA * HD])
                    elif kind == "qT":
                        o = act.copy(sb["mqT"][0:MQ, x[1], :], src[0:MQ, :])
                    elif kind == "krT":
                        o = act.copy(sb["mkT"][HD:MQ, :, :],
                                     src[HD:MQ, :].unsqueeze(1).to_broadcast([ROPE, H_MLA, SEQ]))
                    elif kind == "dqk":
                        o = act.copy(sb["dqkT"][:, x[1], :], src[:, :])
                    elif kind == "dv":
                        o = act.copy(sb["dv"][:, x[2], x[1] * 192:x[1] * 192 + 192], src[:, 0:192])
                    elif kind == "sqk":
                        o = act.copy(sb["sqkT"][:, x[1], :], src[:, :])
                    elif kind == "sv":
                        o = act.copy(sb["sv"][:, x[1], :], src[:, 0:256])
                    o.then_inc(S["unit_out"], 1)
                    if x == ("rest", 1, NT - 1):
                        act.wait_ge(S["unit_out"], u + 1)
                        for t in range(NT):
                            if t:
                                act.wait_ge(S["squares"], 2 * t)
                            act.activation(junk[:, 0:RQ], cq[:, t, :], ACT.Square,
                                           accum_out=ms[:, 0, t:t + 1]).then_inc(S["squares"], 1)
                            act.wait_ge(S["squares"], 2 * t + 1)
                            act.activation(junk[:, 0:RKV], ckv[:, t, :], ACT.Square,
                                           accum_out=ms[:, 1, t:t + 1]).then_inc(S["squares"], 1)
                        act.wait_ge(S["mean_squares"], 2)
                        act.activation(ms[:], ms[:], ACT.Sqrt).then_inc(S["root"], 1)

            @block.vector
            def _(dve):
                steps = 0

                def step(i):
                    nonlocal steps
                    i.then_inc(S["dve_step"], 1)
                    steps += 1
                    dve.wait_ge(S["dve_step"], steps)

                dve.memset(kr[:, :, 0:HD], 0.0).then_inc(S["kr_zero"], 1)
                dve.wait_ge(S["squares"], 2 * NT)
                for j, n in enumerate((RQ, RKV)):
                    dve.tensor_scalar(ms[:, j, :], ms[:, j, :], 1.0 / n, RMS_EPS, ALU.mult, ALU.add
                                      ).then_inc(S["mean_squares"], 1)
                dve.wait_ge(S["root"], 1)
                step(dve.reciprocal(ms[:], ms[:]))
                for t in range(NT):
                    dve.tensor_scalar(cq[:, t, :], cq[:, t, :], ms[:, 0, t:t + 1], None, ALU.mult
                                      ).then_inc(S["latent_ready"], 1)
                    dve.tensor_scalar(ckv[:, t, :], ckv[:, t, :], ms[:, 1, t:t + 1], None, ALU.mult
                                      ).then_inc(S["latent_ready"], 1)
                n = 0
                for i in (3, 2, 1):
                    w = P * (i + 1)
                    sc = score[:, PEN_AT[i]:PEN_AT[i] + w]
                    for g in range(H_IDX):
                        dve.wait_ge(S["unit_out"], place[("idx", i, g)] + 1)
                        if g == 0:
                            o = dve.tensor_scalar(sc, rel[:, n % 2, 0:w], iw(i, g), None, ALU.mult)
                        else:
                            dve.wait_ge(S["rel_used"], n)
                            o = dve.scalar_tensor_tensor(out=sc, in0=rel[:, n % 2, 0:w], scalar=iw(i, g),
                                                         in1=sc, op0=ALU.mult, op1=ALU.add)
                        o.then_inc(S["rel_used"], 1)
                        n += 1
                    dve.wait_ge(S["rel_used"], n)
                    diag = score[:, PEN_AT[i] + w - P:PEN_AT[i] + w]
                    step(dve.tensor_tensor(diag, diag, sb["mask"][:, SEQ - P:SEQ], ALU.add))
                for i in (3, 2, 1):
                    w = P * (i + 1)
                    sc = score[:, PEN_AT[i]:PEN_AT[i] + w]
                    for _ in range(TOPK_KEYS // 8):
                        step(dve.max(top8[:], sc))
                        step(dve.match_replace(sc, top8[:], sc, TAKEN))
                    dve.tensor_scalar(sb["pen"][:, PEN_AT[i]:PEN_AT[i] + w], sc, TAKEN / 2, NEG, ALU.is_gt, ALU.mult)

            @block.gpsimd
            def _(pool):
                steps = 0

                def step(i):
                    nonlocal steps
                    i.then_inc(S["pool_step"], 1)
                    steps += 1
                    pool.wait_ge(S["pool_step"], steps)

                half = ROPE // 2

                def rope(lo, hi, out_lo, out_hi, c, s, r, done):
                    step(pool.tensor_tensor(r[0], lo, s, ALU.mult))
                    step(pool.tensor_tensor(r[1], hi, s, ALU.mult))
                    step(pool.tensor_tensor(out_lo, lo, c, ALU.mult))
                    step(pool.tensor_tensor(out_hi, hi, c, ALU.mult))
                    pool.tensor_tensor(out_lo, out_lo, r[1], ALU.subtract).then_inc(done, 1)
                    pool.tensor_tensor(out_hi, out_hi, r[0], ALU.add).then_inc(done, 1)

                pool.wait_ge(S["unit_out"], place[("rest", 1, NT - 1)] + 1)
                rope(kraw[:, :, 0:half], kraw[:, :, half:ROPE], kr[:, :, HD:HD + half], kr[:, :, HD + half:MQ],
                     cos, sin, [rot[:, j, :, 0, :] for j in range(2)], S["k_roped"])
                pool.wait_ge(S["unit_out"], place[("mq", NT - 1, 1)] + 1)
                bc = lambda a: a.unsqueeze(2).to_broadcast([P, NT, H_MLA, half])
                lo, hi = q_tm[:, :, :, NOPE:NOPE + half], q_tm[:, :, :, NOPE + half:MQ]
                pool.wait_ge(S["k_roped"], 2)
                rope(lo, hi, lo, hi, bc(cos), bc(sin), [rot[:, j] for j in range(2)], S["q_roped"])
        _restart(nc, S)


def _attention(nc, d, sb, l):
    heads = ([("dil", h) for h in range(H_DIL)] + [("mla", h) for h in range(H_MLA)]
             + [("dsa", h) for h in range(H_DSA)])
    column = {"dil": 0, "dsa": H_DIL, "mla": H_DIL + H_DSA}
    units = [(kind, h, i) for kind, h in heads for i in range(NT)]
    NU = len(units)
    NS, NP, NTB = 3, 3, 2
    with ExitStack() as ctx:
        S = _named(ctx, nc, "scores_made logits_out probs_out turned probsT_out heads_made head_out "
                            "pen_added recips w_out_in")
        neg = ctx.enter_context(nc.sbuf_tensor("neg_logits", [P, NS, SEQ], F32))
        probs = ctx.enter_context(nc.sbuf_tensor("probs", [P, NP, SEQ], F32))
        probsT = ctx.enter_context(nc.sbuf_tensor("probsT", [P, NTB, SEQ], F32))
        negmax = ctx.enter_context(nc.sbuf_tensor("negmax", [P, NU], F32))
        total = ctx.enter_context(nc.sbuf_tensor("total", [P, NU], F32))
        recip = ctx.enter_context(nc.sbuf_tensor("recip", [P, NU], F32))
        dsa_bias = ctx.enter_context(nc.sbuf_tensor("dsa_bias", [P, H_DSA, PEN_COLUMNS], F32))
        ps_s = [ctx.enter_context(nc.psum_tensor(f"ps_s{i}", [P, 512], F32)) for i in range(NS)]
        ps_t = [ctx.enter_context(nc.psum_tensor(f"ps_t{i}", [P, 512], F32)) for i in range(NTB)]
        ps_o = [ctx.enter_context(nc.psum_tensor(f"ps_o{i}", [P, NT, P], F32)) for i in range(2)]
        ident = sb["square"][:, 0:P]
        o_sb = sb["o"]
        at = PEN_AT

        def q_of(kind, h, i):
            cols = slice(i * P, (i + 1) * P)
            a = HD * (h % 2)
            if kind == "dil":
                return sb["dqkT"][a:a + HD, h // 2, cols]
            if kind == "dsa":
                return sb["sqkT"][a:a + HD, h // 2, cols]
            return sb["mqT"][0:MQ, h, cols]

        def k_of(kind, h, w):
            a = HD * (h % 2)
            if kind == "dil":
                return sb["dqkT"][a:a + HD, H_DIL // 2 + h // 2, 0:w]
            if kind == "dsa":
                return sb["sqkT"][a:a + HD, H_DSA // 2 + h // 2, 0:w]
            return sb["mkT"][0:MQ, h, 0:w]

        def v_of(kind, h, j):
            return sb[{"dil": "dv", "dsa": "sv", "mla": "mv"}[kind]][:, j, h * HD:(h + 1) * HD]

        def bias_of(kind, h, i):
            w = P * (i + 1)
            if kind == "mla":
                return sb["mask"][:, SEQ - w:SEQ]
            if kind == "dil" or i == 0:
                return sb["bias"][:, h + (H_DIL if kind == "dsa" else 0), SEQ - w:SEQ]
            return dsa_bias[:, h, at[i]:at[i] + w]

        with nc.Block() as block:
            @block.sync
            def _(sp):
                sp.dma_start(sb["w_out"][:], d["w_out"][bass.ds(l, 1)].rearrange("o (p k) c -> p (o k) c", k=KD)
                             ).then_inc(S["w_out_in"], 16)
                sp.wait_ge(S["w_out_in"], 16)

            @block.tensor
            def _(pe):
                def scores(u):
                    kind, h, i = units[u]
                    w = P * (i + 1)
                    if u >= NS:
                        pe.wait_ge(S["logits_out"], u - NS + 1)
                    pe.matmul(ps_s[u % NS][:, 0:w], q_of(kind, h, i), k_of(kind, h, w),
                              start=True, stop=True).then_inc(S["scores_made"], 1)

                def turn(u):
                    kind, h, i = units[u]
                    pe.wait_ge(S["probs_out"], u + 1)
                    for j in range(i + 1):
                        mm = pe.transpose(ps_t[u % NTB][:, j * P:(j + 1) * P], probs[:, u % NP, j * P:(j + 1) * P], ident)
                    mm.then_inc(S["turned"], 1)

                def values(u):
                    kind, h, i = units[u]
                    pe.wait_ge(S["probsT_out"], u + 1)
                    n = u // NT
                    if i == 0 and n >= 2:
                        pe.wait_ge(S["head_out"], n - 1)
                    for j in range(i + 1):
                        mm = pe.matmul(ps_o[n % 2][:, i, 0:HD], probsT[:, u % NTB, j * P:(j + 1) * P],
                                       v_of(kind, h, j), start=(j == 0), stop=(j == i))
                    mm.then_inc(S["heads_made"], 1)

                scores(0)
                scores(1)
                for u in range(NU):
                    if u + 2 < NU:
                        scores(u + 2)
                    turn(u)
                    if u >= 1:
                        values(u - 1)
                values(NU - 1)

            @block.vector
            def _(dve):
                def head_out(n):
                    kind, h = heads[n]
                    dve.wait_ge(S["probs_out"], NT * (n + 1))
                    dve.reciprocal(recip[:, NT * n:NT * n + NT], total[:, NT * n:NT * n + NT]).then_inc(S["recips"], 1)
                    dve.wait_ge(S["recips"], n + 1)
                    dve.wait_ge(S["heads_made"], NT * (n + 1))
                    c = (column[kind] + h) * HD
                    dve.tensor_tensor(o_sb[:, :, c:c + HD], ps_o[n % 2][:, :, 0:HD],
                                      recip[:, NT * n:NT * n + NT].unsqueeze(2).to_broadcast([P, NT, HD]),
                                      ALU.mult).then_inc(S["head_out"], 1)

                for u, (kind, h, i) in enumerate(units):
                    w = P * (i + 1)
                    dve.wait_ge(S["scores_made"], u + 1)
                    if u >= NS:
                        dve.wait_ge(S["probs_out"], u - NS + 1)
                    if kind == "dsa" and i:
                        dve.wait_ge(S["pen_added"], 3 * h + i)
                    dve.tensor_tensor_reduce(neg[:, u % NS, 0:w], ps_s[u % NS][:, 0:w], bias_of(kind, h, i),
                                             -(MLA_SCALE if kind == "mla" else SCALE), 3e38, ALU.add, ALU.min,
                                             negmax[:, u:u + 1]).then_inc(S["logits_out"], 1)
                    if i == 2 and u > NT:
                        head_out(u // NT - 1)
                head_out(len(heads) - 1)

            @block.scalar
            def _(act):
                def probs_t(u):
                    w = P * (units[u][2] + 1)
                    act.wait_ge(S["turned"], u + 1)
                    if u >= NTB:
                        act.wait_ge(S["heads_made"], u - NTB + 1)
                    act.copy(probsT[:, u % NTB, 0:w], ps_t[u % NTB][:, 0:w]).then_inc(S["probsT_out"], 1)

                for u, (kind, h, i) in enumerate(units):
                    w = P * (i + 1)
                    act.wait_ge(S["logits_out"], u + 1)
                    if u >= NP:
                        act.wait_ge(S["turned"], u - NP + 1)
                    act.activation(probs[:, u % NP, 0:w], neg[:, u % NS, 0:w], ACT.Exp, bias=negmax[:, u:u + 1],
                                   scale=-1.0, accum_out=total[:, u:u + 1]).then_inc(S["probs_out"], 1)
                    if u >= 1:
                        probs_t(u - 1)
                probs_t(NU - 1)

            @block.gpsimd
            def _(pool):
                for h in range(H_DSA):
                    for i in range(1, NT):
                        w = P * (i + 1)
                        pool.tensor_tensor(dsa_bias[:, h, at[i]:at[i] + w], sb["bias"][:, H_DIL + h, SEQ - w:SEQ],
                                           sb["pen"][:, PEN_AT[i]:PEN_AT[i] + w], ALU.add).then_inc(S["pen_added"], 1)
        _restart(nc, S)


def _norm_scalar(act, S, r, st, junk, t):
    act.wait_ge(S["mean"], t + 1)
    act.activation(junk[:], r, ACT.Square, bias=st[:, 1, t:t + 1], accum_out=st[:, 2, t:t + 1]).then_inc(S["variance"], 1)
    act.wait_ge(S["variance_eps"], t + 1)
    act.activation(st[:, 3, t:t + 1], st[:, 3, t:t + 1], ACT.Sqrt).then_inc(S["deviation"], 1)


def _norm_vector(dve, S, r, st, gain, shift, out, t, done):
    dve.wait_ge(S["row_sum"], t + 1)
    dve.tensor_scalar(st[:, 1, t:t + 1], st[:, 0, t:t + 1], -1.0 / D, None, ALU.mult).then_inc(S["mean"], 1)
    dve.wait_ge(S["variance"], t + 1)
    dve.tensor_scalar(st[:, 3, t:t + 1], st[:, 2, t:t + 1], 1.0 / D, LN_EPS, ALU.mult, ALU.add).then_inc(S["variance_eps"], 1)
    dve.wait_ge(S["deviation"], t + 1)
    dve.reciprocal(st[:, 4, t:t + 1], st[:, 3, t:t + 1]).then_inc(S["scale"], 1)
    dve.wait_ge(S["scale"], t + 1)
    dve.tensor_scalar(r, r, st[:, 1, t:t + 1], st[:, 4, t:t + 1], ALU.add, ALU.mult).then_inc(S["normed"], 1)
    dve.wait_ge(S["normed"], 2 * t + 1)
    dve.tensor_tensor(r, r, gain[:], ALU.mult).then_inc(S["normed"], 1)
    dve.wait_ge(S["normed"], 2 * t + 2)
    dve.tensor_tensor(out, r, shift[:], ALU.add).then_inc(done, 1)


NORM_SEMS = "row_sum mean variance variance_eps deviation scale normed"


def _place_parts(dve, step, sb):
    step(dve.tensor_copy(sb["parts"][:, 0, :, :, 0], sb["placed"][:]))
    step(dve.tensor_tensor(sb["parts"][:, 1, :, :, 0], sb["placed"][:], sb["parts"][:, 0, :, :, 0], ALU.subtract))


def _mix_and_route(nc, d, sb, l):
    with ExitStack() as ctx:
        S = _named(ctx, nc, NORM_SEMS + " norm_in small_in shared_in oT_made oT_out mixed mix_read x1_ready x1_out x1T_made x1T_out "
                            "logits_made exps up_made silu_out gated down_made acc_ready acc0_out acc1_out "
                            "mask_ready pos_made pos_read route_step  tables")
        T = lambda name, shape, dt=F32: ctx.enter_context(nc.sbuf_tensor(name, shape, dt))
        oT = T("oT", [P, 2, KD, P])
        r = T("r", [P, 2, D])
        junk = T("junk3", [P, D])
        st = T("st3", [P, 5, NT])
        gain, shift = T("gain1", [P, D]), T("shift1", [P, D])
        x1T = T("x1T", [P, KD, SEQ])
        rw = T("rw", [P, KD, NE])
        rb = T("rb", [P, NE])
        w13 = T("sh_w13", [P, 2, KD, SFF])
        w2 = T("sh_w2_sb", [P, 2, D])
        act_out = T("sh_silu", [P, 2, SEQ])
        shT = T("shT", [P, 2, SEQ])
        acc = T("acc_sb", [P, 2, D])
        e, s, sel, left, mask, gate = (T(n, [P, NT, NE]) for n in ("e", "s", "sel", "left", "picked", "gate_raw"))
        top8 = T("top8r", [P, NT, 8])
        gsum = T("gsum", [P, 2, NT])
        cnt = T("cnt", [P, MAX_PASSES])
        ps = lambda name, shape: ctx.enter_context(nc.psum_tensor(name, shape, F32))
        ps_a, ps_mix, ps_x = ps("ps_a", [P, KD, P]), ps("ps_mix", [P, D]), ps("ps_x", [P, KD, P])
        ps_r, ps_c = ps("ps_r", [P, 2, NT, NE]), ps("ps_c", [P, 512])
        flat_a, flat_x = (q[:].rearrange("p k c -> p (k c)") for q in (ps_a, ps_x))
        square = sb["square"]
        ident, earlier, ones = square[:, 0:P], square[:, P:2 * P], square[:, 2 * P:3 * P]
        x_sb, o_sb = sb["x"], sb["o"]
        up_bank = [flat_a[:, 0:512], flat_a[:, 512:1024], flat_x[:, 0:512], flat_x[:, 512:1024]]
        dn_bank = [ps_mix[:, :], flat_a]

        with nc.Block() as block:
            @block.sync
            def _(sp):
                row = lambda name, n: d[name][bass.ds(l, 1)].to_broadcast([P, n])
                sp.dma_start(gain[:], row("ln1_g", D)).then_inc(S["norm_in"], 16)
                sp.dma_start(shift[:], row("ln1_b", D)).then_inc(S["norm_in"], 16)
                sp.dma_start(rb[:], row("router_bias", NE)).then_inc(S["small_in"], 16)
                sp.dma_start(rw[:], d["router_w"][bass.ds(l, 1)].rearrange("o (p k) e -> p (o k) e", k=KD)).then_inc(S["small_in"], 16)
                for j, name in enumerate(("sh_w1", "sh_w3")):
                    sp.dma_start(w13[:, j], d[name][bass.ds(l, 1)].rearrange("o (p k) f -> p (o k) f", k=KD)).then_inc(S["shared_in"], 16)
                sp.dma_start(w2[:], d["sh_w2"][bass.ds(l, 1)].rearrange("o (m p) c -> p (o m) c", p=P)).then_inc(S["shared_in"], 16)
                for t in range(NT):
                    sp.wait_ge(S["x1_ready"], t + 1)
                    sp.dma_start(d["x1_rows"][t * P:(t + 1) * P, :], x_sb[:, t, :]).then_inc(S["x1_out"], 16)
                for t in range(NT):
                    sp.wait_ge(S["acc_ready"], t + 1)
                    sp.dma_start(d["acc_rows"][t * P:(t + 1) * P, :], acc[:, t % 2, :]).then_inc(S[f"acc{t % 2}_out"], 16)
                sp.wait_ge(S["x1_out"], 64)
                for b in range(2):
                    sp.wait_ge(S[f"acc{b}_out"], 32)

            @block.tensor
            def _(pe):
                def turn_o(t):
                    if t:
                        pe.wait_ge(S["oT_out"], t)
                    for k in range(KD):
                        mm = pe.transpose(ps_a[:, k, :], o_sb[:, t, k::KD], ident)
                    mm.then_inc(S["oT_made"], 1)

                def mix(t):
                    pe.wait_ge(S["oT_out"], t + 1)
                    if t:
                        pe.wait_ge(S["row_sum"], t)
                    for c in range(2):
                        for k in range(KD):
                            mm = pe.matmul(ps_mix[:, c * 512:(c + 1) * 512], oT[:, t % 2, k, :],
                                           sb["w_out"][:, k, c * 512:(c + 1) * 512], start=(k == 0), stop=(k == KD - 1))
                    mm.then_inc(S["mixed"], 1)

                def turn_x(t):
                    pe.wait_ge(S["x1_ready"], t + 1)
                    if t:
                        pe.wait_ge(S["x1T_out"], t)
                    for k in range(KD):
                        mm = pe.transpose(ps_x[:, k, :], x_sb[:, t, k::KD], ident)
                    mm.then_inc(S["x1T_made"], 1)

                def router(t):
                    pe.wait_ge(S["x1T_out"], t + 1)
                    pe.wait_ge(S["small_in"], 32)
                    for k in range(KD):
                        mm = pe.matmul(ps_r[:, 0, t, :], x1T[:, k, t * P:(t + 1) * P], rw[:, k, :],
                                       start=(k == 0), stop=(k == KD - 1))
                    mm.then_inc(S["logits_made"], 1)

                turn_o(0)
                for t in range(NT):
                    mix(t)
                    if t + 1 < NT:
                        turn_o(t + 1)
                    if t >= 2:
                        turn_x(t - 2)
                        router(t - 2)
                for t in (NT - 2, NT - 1):
                    turn_x(t)
                    router(t)
                pe.wait_ge(S["shared_in"], 48)
                for q in range(4):
                    for k in range(KD):
                        mm = pe.matmul(up_bank[q], w13[:, q // 2, k, (q % 2) * P:(q % 2 + 1) * P], x1T[:, k, :],
                                       start=(k == 0), stop=(k == KD - 1))
                    mm.then_inc(S["up_made"], 1)
                pe.wait_ge(S["mask_ready"], 1)
                for t in range(NT):
                    for q in range(t):
                        pe.matmul(ps_r[:, 1, t, :], ones, mask[:, q, :], start=(q == 0), stop=False)
                    mm = pe.matmul(ps_r[:, 1, t, :], earlier, mask[:, t, :], start=(t == 0), stop=True)
                for t in range(NT):
                    mm = pe.matmul(ps_c[:, 0:NE], ones, mask[:, t, :], start=(t == 0), stop=(t == NT - 1))
                mm.then_inc(S["pos_made"], 1)
                pe.wait_ge(S["gated"], 2)
                for t in range(NT):
                    if t >= 2:
                        pe.wait_ge(S["acc_ready"], t - 1)
                    for c in range(2):
                        for m in range(2):
                            mm = pe.matmul(dn_bank[t % 2][:, c * 512:(c + 1) * 512], shT[:, m, t * P:(t + 1) * P],
                                           w2[:, m, c * 512:(c + 1) * 512], start=(m == 0), stop=(m == 1))
                    mm.then_inc(S["down_made"], 1)

            @block.scalar
            def _(act):
                def copy_o(t):
                    act.wait_ge(S["oT_made"], t + 1)
                    if t >= 2:
                        act.wait_ge(S["mixed"], t - 1)
                    act.copy(oT[:, t % 2].rearrange("p k c -> p (k c)"), flat_a).then_inc(S["oT_out"], 1)

                def copy_x(t):
                    act.wait_ge(S["x1T_made"], t + 1)
                    act.copy(x1T[:, :, t * P:(t + 1) * P], ps_x[:]).then_inc(S["x1T_out"], 1)

                copy_o(0)
                for t in range(NT):
                    if t + 1 < NT:
                        copy_o(t + 1)
                    if t:
                        act.wait_ge(S["variance"], t)
                    _norm_scalar(act, S, r[:, t % 2, :], st, junk, t)
                    if t >= 2:
                        copy_x(t - 2)
                copy_x(NT - 2)
                copy_x(NT - 1)
                act.wait_ge(S["logits_made"], NT)
                act.activation(e[:], ps_r[:, 0], ACT.Exp, scale=-1.0).then_inc(S["exps"], 1)
                for m in range(2):
                    act.wait_ge(S["up_made"], m + 1)
                    act.activation(act_out[:, m, :], up_bank[m], ACT.Silu).then_inc(S["silu_out"], 1)

            @block.vector
            def _(dve):
                steps = 0

                def step(i):
                    nonlocal steps
                    i.then_inc(S["route_step"], 1)
                    steps += 1
                    dve.wait_ge(S["route_step"], steps)

                dve.wait_ge(S["norm_in"], 32)
                for t in range(NT):
                    dve.wait_ge(S["mixed"], t + 1)
                    if t >= 2:
                        dve.wait_ge(S["x1_ready"], t - 1)
                    dve.scalar_tensor_tensor(out=r[:, t % 2, :], in0=x_sb[:, t, :], scalar=ALPHA, in1=ps_mix[:, :],
                                             op0=ALU.mult, op1=ALU.add, accum_out=st[:, 0, t:t + 1]
                                             ).then_inc(S["row_sum"], 1)
                    _norm_vector(dve, S, r[:, t % 2, :], st, gain, shift, x_sb[:, t, :], t, S["x1_ready"])
                dve.wait_ge(S["exps"], 1)
                dve.wait_ge(S["small_in"], 32)
                step(dve.tensor_scalar(e[:], e[:], 1.0, None, ALU.add))
                step(dve.reciprocal(s[:], e[:]))
                step(dve.tensor_tensor(sel[:], s[:], rb[:].unsqueeze(1).to_broadcast([P, NT, NE]), ALU.add))
                for t in range(NT):
                    step(dve.max(top8[:, t, :], sel[:, t, :]))
                    step(dve.match_replace(left[:, t, :], top8[:, t, :], sel[:, t, :], NEG))
                dve.tensor_scalar(mask[:], left[:], NEG / 10, None, ALU.is_lt).then_inc(S["mask_ready"], 1)
                dve.wait_ge(S["mask_ready"], 1)
                step(dve.tensor_tensor(gate[:], s[:], mask[:], ALU.mult))
                step(dve.tensor_reduce(gsum[:, 0, :], gate[:], AX.X, ALU.add))
                step(dve.reciprocal(gsum[:, 1, :], gsum[:, 0, :]))
                step(dve.tensor_scalar(gsum[:, 0, :], gsum[:, 1, :], ROUTED_SCALE, None, ALU.mult))
                step(dve.tensor_tensor(gate[:], gate[:], gsum[:, 0, :].unsqueeze(2).to_broadcast([P, NT, NE]), ALU.mult))
                for q in range(3):
                    step(dve.tensor_copy(sb["parts"][:, q, :, :, 1], gate[:]))
                    if q < 2:
                        step(dve.tensor_tensor(gate[:], gate[:], sb["parts"][:, q, :, :, 1], ALU.subtract))
                dve.memset(sb["parts"][:, 2, :, :, 0], 0.0).then_inc(S["tables"], 1)
                for m in range(2):
                    dve.wait_ge(S["silu_out"], m + 1)
                    dve.wait_ge(S["up_made"], m + 3)
                    dve.tensor_tensor(shT[:, m, :], up_bank[m + 2], act_out[:, m, :], ALU.mult).then_inc(S["gated"], 1)
                dve.wait_ge(S["pos_made"], 1)
                posm = sb["posm"][:, :, 0:NE]
                step(dve.scalar_tensor_tensor(out=posm, in0=ps_r[:, 1], scalar=NOT_ROUTED, in1=mask[:],
                                              op0=ALU.add, op1=ALU.mult))
                step(dve.tensor_scalar(posm, posm, NOT_ROUTED, None, ALU.subtract))
                placed = sb["placed"]
                for t in range(NT):
                    step(dve.tensor_scalar(placed[:, t, :], posm[:, t, :], -1.0,
                                           sb["row"][:, ROPE // 2 + 1 + t:ROPE // 2 + 2 + t], ALU.mult, ALU.add))
                _place_parts(dve, step, sb)
                step(dve.tensor_reduce(cnt[:, 0:1], ps_c[:, 0:NE], AX.X, ALU.max))
                step(dve.tensor_scalar(cnt[:, 1:2], cnt[:, 0:1], float(CAP), 1.0, ALU.is_gt, ALU.add))
                for q in range(2, MAX_PASSES):
                    step(dve.scalar_tensor_tensor(out=cnt[:, q:q + 1], in0=cnt[:, 0:1], scalar=float(q * CAP),
                                                  in1=cnt[:, q - 1:q], op0=ALU.is_gt, op1=ALU.add))
                step(dve.tensor_copy(sb["passes"][:], cnt[:, MAX_PASSES - 1:MAX_PASSES]))
                for t in range(NT):
                    dve.wait_ge(S["down_made"], t + 1)
                    if t >= 2:
                        dve.wait_ge(S[f"acc{t % 2}_out"], 16 * (t // 2))
                    dve.scalar_tensor_tensor(out=acc[:, t % 2, :], in0=x_sb[:, t, :], scalar=ALPHA, in1=dn_bank[t % 2],
                                             op0=ALU.mult, op1=ALU.add).then_inc(S["acc_ready"], 1)
        _restart(nc, S)


SLOTS = 4


class Turn:

    def __init__(self, lap, slot):
        self.lap, self.slot = lap, slot
        self.n = lap * SLOTS + slot
        self.known = isinstance(lap, int)

    def __add__(self, k):
        s = self.slot + k
        return Turn(self.lap + s // SLOTS, s % SLOTS)

    def has(self, k):
        return not self.known or 0 <= self.n + k < NE


def _laps(eng, step):
    for s in range(SLOTS):
        step(Turn(0, s))
    with eng.Fori(1, NE // SLOTS - 1) as lap:
        for s in range(SLOTS):
            step(Turn(lap, s))
    for s in range(SLOTS):
        step(Turn(NE // SLOTS - 1, s))


def _experts(nc, d, sb, l):
    with ExitStack() as ctx:
        S = _named(ctx, nc, "up0_in up1_in up2_in up3_in dn0_in dn1_in dn2_in dn3_in hot_ready picked_made index_ready "
                            "rows0_in rows1_in rows_turned rowsT_a rowsT_b up_made silu_out hidden_ready hidden_turned "
                            "hiddenT_out down_made y_a y_b added shifted dma_turns")
        T = lambda name, shape, dt=F32: ctx.enter_context(nc.sbuf_tensor(name, shape, dt))
        w13 = T("w13", [P, SLOTS, 2, KD, FF])
        w2 = T("w2", [P, SLOTS, 2, D])
        hot = T("hot", [P, 2, NT, CAP], BF16)
        index = T("index", [P, SLOTS], I32)
        y_index = T("y_index", [P, SLOTS], I32)
        gate = T("gate", [P, SLOTS])
        rows = T("rows", [P, 2, D])
        rowsT = T("rowsT", [P, 2, KD, CAP])
        silu = T("silu", [P, 2, FF])
        hidden = T("hidden", [P, 2, FF])
        hiddenT = T("hiddenT", [P, 2, 2, CAP])
        y = T("y", [P, SLOTS, D])
        ps = lambda name, shape: ctx.enter_context(nc.psum_tensor(name, shape, F32))
        ps_up = [ps(f"ps_up{i}", [P, 2, FF]) for i in range(2)]
        ps_t, ps_y = ps("ps_t", [P, KD, P]), ps("ps_y", [P, D])
        ps_h, ps_p = ps("ps_h", [P, 4, P]), ps("ps_p", [P, 512])
        ident = sb["square"][:, 0:P]
        ident_cap = sb["square"][0:CAP, 0:CAP]
        number = sb["number"][:]
        pad_row = sb["row"][0:CAP, ROPE // 2:ROPE // 2 + 1]
        posm = sb["posm"]
        HALF = KD // 2

        with nc.Block() as block:
            @block.sync
            def _(sp):
                w1 = d["exp_w1"].rearrange("l e (p k) f -> (l e) p k f", k=KD)
                w3 = d["exp_w3"].rearrange("l e (p k) f -> (l e) p k f", k=KD)
                w2d = d["exp_w2"].rearrange("l e (p j) c -> (l e) p j c", j=2)

                def load(x):
                    e = bass.ds(l * NE + x.n, 1)
                    if x.has(-SLOTS):
                        sp.wait_ge(S["up_made"], x.n - SLOTS + 1)
                    sp.dma_start(w13[:, x.slot, 0], w1[e].rearrange("o p k f -> p (o k) f")).then_inc(S[f"up{x.slot}_in"], 16)
                    sp.dma_start(w13[:, x.slot, 1], w3[e].rearrange("o p k f -> p (o k) f")).then_inc(S[f"up{x.slot}_in"], 16)
                    if x.has(-SLOTS):
                        sp.wait_ge(S["down_made"], x.n - SLOTS + 1)
                    sp.dma_start(w2[:, x.slot], w2d[e].rearrange("o p j c -> p (o j) c")).then_inc(S[f"dn{x.slot}_in"], 16)

                _laps(sp, load)

            @block.gpsimd
            def _(pool):
                def gather(x):
                    b = x.slot % 2
                    pool.wait_ge(S["index_ready"], x.n + 1)
                    if x.has(-2):
                        pool.wait_ge(S["rows_turned"], x.n - 1)
                    pool.sem_inc(S["dma_turns"], 1)
                    pool.indirect_dma_start(rows[0:CAP, b, :], None, d["x1_rows"],
                                            bass.IndirectOffsetOnAxis(ap=index[0:CAP, x.slot:x.slot + 1], axis=0)
                                            ).then_inc(S[f"rows{b}_in"], 16)

                def add(x):
                    pool.wait_ge(S["y_a"], x.n + 1)
                    pool.wait_ge(S["y_b"], x.n + 1)
                    if x.has(-1):
                        pool.wait_ge(S["added"], 16 * x.n)
                    pool.sem_inc(S["dma_turns"], 1)
                    pool.indirect_dma_start(d["acc_rows"], bass.IndirectOffsetOnAxis(ap=y_index[0:CAP, x.slot:x.slot + 1], axis=0),
                                            y[0:CAP, x.slot, :], None, compute_op=ALU.add).then_inc(S["added"], 16)

                gather(Turn(0, 0))
                gather(Turn(0, 1))

                def step(x):
                    if x.has(-2):
                        add(x + -2)
                    if x.has(2):
                        gather(x + 2)
                _laps(pool, step)
                add(Turn(NE // SLOTS - 1, SLOTS - 2))
                add(Turn(NE // SLOTS - 1, SLOTS - 1))
                pool.wait_ge(S["added"], 16 * NE)

            @block.tensor
            def _(pe):
                def pick(x):
                    b = x.slot % 2
                    pe.wait_ge(S["hot_ready"], x.n + 1)
                    if x.has(-1):
                        pe.wait_ge(S["index_ready"], x.n)
                    for t in range(NT):
                        for q in range(3):
                            mm = pe.matmul(ps_p[0:CAP, 0:2], hot[:, b, t, :],
                                           sb["parts"][:, q, t, bass.ds(x.n, 1), :].rearrange("p o v -> p (o v)"),
                                           start=(t == 0 and q == 0), stop=(t == NT - 1 and q == 2))
                    mm.then_inc(S["picked_made"], 1)

                def turn_rows(x):
                    b = x.slot % 2
                    pe.wait_ge(S[f"rows{b}_in"], 16 * (x.lap * (SLOTS // 2) + x.slot // 2 + 1))
                    if x.has(-1):
                        pe.wait_ge(S["rowsT_a"], x.n)
                        pe.wait_ge(S["rowsT_b"], x.n)
                    for k in range(KD):
                        mm = pe.transpose(ps_t[:, k, 0:CAP], rows[0:CAP, b, k::KD], ident_cap)
                    mm.then_inc(S["rows_turned"], 1)

                def up(x, part):
                    b = x.slot % 2
                    if part == 0:
                        pe.wait_ge(S[f"up{x.slot}_in"], 32 * (x.lap + 1))
                        pe.wait_ge(S["rowsT_a"], x.n + 1)
                        pe.wait_ge(S["rowsT_b"], x.n + 1)
                        if x.has(-2):
                            pe.wait_ge(S["hidden_ready"], x.n - 1)
                    for k in range(HALF * part, HALF * part + HALF):
                        mm = pe.matmul(ps_up[b][0:CAP], rowsT[:, b, k, :], w13[:, x.slot, :, k, :],
                                       start=(k == 0), stop=(k == KD - 1))
                    if part:
                        mm.then_inc(S["up_made"], 1)

                def turn_hidden(x):
                    b = x.slot % 2
                    pe.wait_ge(S["hidden_ready"], x.n + 1)
                    if x.has(-1):
                        pe.wait_ge(S["hiddenT_out"], x.n)
                    for j in range(2):
                        mm = pe.transpose(ps_h[:, j, 0:CAP], hidden[0:CAP, b, j::2], ident_cap)
                    mm.then_inc(S["hidden_turned"], 1)

                def down(x):
                    b = x.slot % 2
                    pe.wait_ge(S[f"dn{x.slot}_in"], 16 * (x.lap + 1))
                    pe.wait_ge(S["hiddenT_out"], x.n + 1)
                    if x.has(-1):
                        pe.wait_ge(S["y_a"], x.n)
                        pe.wait_ge(S["y_b"], x.n)
                    for c in range(2):
                        for j in range(2):
                            mm = pe.matmul(ps_y[0:CAP, c * 512:(c + 1) * 512], hiddenT[:, b, j, :],
                                           w2[:, x.slot, j, c * 512:(c + 1) * 512], start=(j == 0), stop=(j == 1))
                    mm.then_inc(S["down_made"], 1)

                pick(Turn(0, 0))
                pick(Turn(0, 1))
                turn_rows(Turn(0, 0))

                def step(x):
                    if x.has(2):
                        pick(x + 2)
                    up(x, 0)
                    if x.has(-1):
                        turn_hidden(x + -1)
                    up(x, 1)
                    if x.has(1):
                        turn_rows(x + 1)
                    if x.has(-1):
                        down(x + -1)
                _laps(pe, step)
                last = Turn(NE // SLOTS - 1, SLOTS - 1)
                turn_hidden(last)
                down(last)

            @block.vector
            def _(dve):
                def hots(x):
                    b = x.slot % 2
                    if x.has(-2):
                        dve.wait_ge(S["picked_made"], x.n - 1)
                    for t in range(NT):
                        o = dve.tensor_scalar(hot[:, b, t, :], number, posm[:, t, bass.ds(x.n, 1)], None, ALU.is_equal)
                    o.then_inc(S["hot_ready"], 1)

                def indices(x):
                    b = x.slot % 2
                    dve.wait_ge(S["picked_made"], x.n + 1)
                    if x.has(-SLOTS):
                        dve.wait_ge(S["rows_turned"], x.n - SLOTS + 1)
                        dve.wait_ge(S["y_a"], x.n - SLOTS + 1)
                        dve.wait_ge(S["y_b"], x.n - SLOTS + 1)
                    dve.tensor_copy(gate[0:CAP, x.slot:x.slot + 1], ps_p[0:CAP, 1:2])
                    dve.tensor_scalar(index[0:CAP, x.slot:x.slot + 1], ps_p[0:CAP, 0:1], pad_row, None, ALU.add
                                      ).then_inc(S["index_ready"], 1)

                def hide(x):
                    b = x.slot % 2
                    dve.wait_ge(S["silu_out"], x.n + 1)
                    if x.has(-2):
                        dve.wait_ge(S["hidden_turned"], x.n - 1)
                    dve.tensor_tensor(hidden[0:CAP, b, :], ps_up[b][0:CAP, 1, :], silu[0:CAP, b, :], ALU.mult
                                      ).then_inc(S["hidden_ready"], 1)

                def rows_a(x):
                    dve.wait_ge(S["rows_turned"], x.n + 1)
                    if x.has(-2):
                        dve.wait_ge(S["up_made"], x.n - 1)
                    dve.tensor_copy(rowsT[:, x.slot % 2, 0:HALF, :], ps_t[:, 0:HALF, 0:CAP]).then_inc(S["rowsT_a"], 1)

                def y_first(x):
                    dve.wait_ge(S["down_made"], x.n + 1)
                    dve.wait_ge(S["index_ready"], x.n + 1)
                    if x.has(-SLOTS):
                        dve.wait_ge(S["added"], 16 * (x.n - SLOTS + 1))
                    dve.tensor_scalar(y[0:CAP, x.slot, 0:512], ps_y[0:CAP, 0:512], gate[0:CAP, x.slot:x.slot + 1], None,
                                      ALU.mult)
                    dve.tensor_copy(y_index[0:CAP, x.slot:x.slot + 1], index[0:CAP, x.slot:x.slot + 1]).then_inc(S["y_a"], 1)

                hots(Turn(0, 0))
                hots(Turn(0, 1))
                indices(Turn(0, 0))
                indices(Turn(0, 1))
                hots(Turn(0, 2))
                rows_a(Turn(0, 0))

                def step(x):
                    if x.has(3):
                        hots(x + 3)
                    if x.has(2):
                        indices(x + 2)
                    hide(x)
                    if x.has(1):
                        rows_a(x + 1)
                    if x.has(-1):
                        y_first(x + -1)
                _laps(dve, step)
                y_first(Turn(NE // SLOTS - 1, SLOTS - 1))
                dve.wait_ge(S["hot_ready"], NE)
                dve.wait_ge(S["picked_made"], NE)
                shifts = 0

                def step(i):
                    nonlocal shifts
                    i.then_inc(S["shifted"], 1)
                    shifts += 1
                    dve.wait_ge(S["shifted"], shifts)

                step(dve.tensor_scalar(posm[:], posm[:], float(CAP), None, ALU.subtract))
                step(dve.tensor_scalar(sb["placed"][:], sb["placed"][:], float(CAP), None, ALU.add))
                _place_parts(dve, step, sb)

            @block.scalar
            def _(act):
                def rows_b(x):
                    act.wait_ge(S["rows_turned"], x.n + 1)
                    if x.has(-2):
                        act.wait_ge(S["up_made"], x.n - 1)
                    act.copy(rowsT[:, x.slot % 2, HALF:KD, :], ps_t[:, HALF:KD, 0:CAP]).then_inc(S["rowsT_b"], 1)

                def hidden_t(x):
                    act.wait_ge(S["hidden_turned"], x.n + 1)
                    if x.has(-2):
                        act.wait_ge(S["down_made"], x.n - 1)
                    act.copy(hiddenT[:, x.slot % 2], ps_h[:, 0:2, 0:CAP]).then_inc(S["hiddenT_out"], 1)

                def gates(x):
                    act.wait_ge(S["up_made"], x.n + 1)
                    if x.has(-2):
                        act.wait_ge(S["hidden_ready"], x.n - 1)
                    act.activation(silu[0:CAP, x.slot % 2, :], ps_up[x.slot % 2][0:CAP, 0, :], ACT.Silu).then_inc(S["silu_out"], 1)

                def y_second(x):
                    act.wait_ge(S["down_made"], x.n + 1)
                    act.wait_ge(S["index_ready"], x.n + 1)
                    if x.has(-SLOTS):
                        act.wait_ge(S["added"], 16 * (x.n - SLOTS + 1))
                    act.activation(y[0:CAP, x.slot, 512:D], ps_y[0:CAP, 512:D], ACT.Copy, scale=gate[0:CAP, x.slot:x.slot + 1]
                                   ).then_inc(S["y_b"], 1)

                rows_b(Turn(0, 0))

                def step(x):
                    if x.has(-1):
                        hidden_t(x + -1)
                    gates(x)
                    if x.has(1):
                        rows_b(x + 1)
                    if x.has(-1):
                        y_second(x + -1)
                _laps(act, step)
                last = Turn(NE // SLOTS - 1, SLOTS - 1)
                hidden_t(last)
                y_second(last)
        _restart(nc, S)


def _second_norm(nc, d, sb, l):
    with ExitStack() as ctx:
        S = _named(ctx, nc, NORM_SEMS + " norm_in acc0_in acc1_in acc2_in acc3_in x_ready")
        acc = ctx.enter_context(nc.sbuf_tensor("acc5", [P, NT, D], F32))
        junk = ctx.enter_context(nc.sbuf_tensor("junk5", [P, D], F32))
        st = ctx.enter_context(nc.sbuf_tensor("st5", [P, 5, NT], F32))
        gain = ctx.enter_context(nc.sbuf_tensor("gain2", [P, D], F32))
        shift = ctx.enter_context(nc.sbuf_tensor("shift2", [P, D], F32))
        with nc.Block() as block:
            @block.sync
            def _(sp):
                for t in range(NT):
                    sp.dma_start(acc[:, t, :], d["acc_rows"][t * P:(t + 1) * P, :]).then_inc(S[f"acc{t}_in"], 16)
                    if t == 0:
                        for tile, name in ((gain, "ln2_g"), (shift, "ln2_b")):
                            sp.dma_start(tile[:], d[name][bass.ds(l, 1)].to_broadcast([P, D])).then_inc(S["norm_in"], 16)

            @block.scalar
            def _(act):
                for t in range(NT):
                    if t:
                        act.wait_ge(S["variance"], t)
                    _norm_scalar(act, S, acc[:, t, :], st, junk, t)

            @block.vector
            def _(dve):
                for t in range(NT):
                    dve.wait_ge(S[f"acc{t}_in"], 16)
                    dve.tensor_reduce(st[:, 0, t:t + 1], acc[:, t, :], AX.X, ALU.add).then_inc(S["row_sum"], 1)
                    if t == 0:
                        dve.wait_ge(S["norm_in"], 32)
                    _norm_vector(dve, S, acc[:, t, :], st, gain, shift, sb["x"][:, t, :], t, S["x_ready"])
        _restart(nc, S)


def trunk(nc, d, out):
    with ExitStack() as ctx:
        T = lambda name, shape, dt=F32: ctx.enter_context(nc.sbuf_tensor(name, shape, dt))
        d["x1_rows"] = nc.dram_tensor("x1_rows", [ACC_ROWS, D], F32).ap()
        d["acc_rows"] = nc.dram_tensor("acc_rows", [ACC_ROWS, D], F32).ap()
        d["bias_rows"] = nc.dram_tensor("bias_rows", [10, SPAN + 1], F32).ap()
        sb = {"x": T("x_sb", [P, NT, D]), "xT": T("xT", [P, KD, SEQ]), "bias": T("bias", [P, 10, SEQ]),
              "mask": T("mask", [P, SEQ]), "square": T("square", [P, 3 * P]),
              "row": T("row", [P, ROPE // 2 + 1 + NT]), "rope": T("rope", [P, NT, 2, ROPE // 2]),
              "posm": T("posm", [P, NT, NE]), "placed": T("placed", [P, NT, NE]), "parts": T("parts", [P, 3, NT, NE, 2], BF16),
              "number": T("number", [P, CAP], BF16), "passes": T("passes", [P, 1], I32)}
        sb["o"] = sb["xT"][:].rearrange("p k c -> p (k c)").rearrange("p (t c) -> p t c", t=NT)
        out_stored = ctx.enter_context(nc.semaphore("out_stored"))
        _setup(nc, d, sb)
        with nc.Fori(0, DEPTH) as l:
            with ExitStack() as late:
                with ExitStack() as mixer:
                    M = lambda name, shape: mixer.enter_context(nc.sbuf_tensor(name, shape, F32))
                    sb |= {"dqkT": M("dqkT", [P, 6, SEQ]), "sqkT": M("sqkT", [P, 4, SEQ]),
                           "dv": M("dv", [P, NT, H_DIL * HD]), "sv": M("sv", [P, NT, H_DSA * HD]),
                           "mqT": M("mqT", [P, H_MLA, SEQ]), "mkT": M("mkT", [P, H_MLA, SEQ]),
                           "mv": M("mv", [P, NT, H_MLA * HD]), "pen": M("pen", [P, PEN_COLUMNS])}
                    _projections(nc, d, sb, l)
                    sb["w_out"] = late.enter_context(nc.sbuf_tensor("w_out_sb", [P, KD, D], F32, side="right"))
                    _attention(nc, d, sb, l)
                _mix_and_route(nc, d, sb, l)
            passes = nc.values_load(sb["passes"][0:1, 0:1], min_val=1, max_val=MAX_PASSES)
            with nc.Fori(0, passes) as _:
                _experts(nc, d, sb, l)
            _second_norm(nc, d, sb, l)
        with nc.Block() as block:
            @block.sync
            def _(sp):
                sp.dma_start(out.rearrange("o (t p) m -> p (o t) m", p=P), sb["x"][:]).then_inc(out_stored, 16)
                sp.wait_ge(out_stored, 16)


_INS = ["x", "positions", "w_in", "mla_q_norm", "mla_w_uq", "mla_kv_norm", "mla_w_ukv", "w_out", "ln1_g", "ln1_b",
        "router_w", "router_bias", "exp_w1", "exp_w3", "exp_w2", "sh_w1", "sh_w3", "sh_w2", "ln2_g", "ln2_b", "rel_bias"]


def kernel(**inputs):
    import concourse.bacc as _bacc
    from concourse.bass_utils import run_bass_kernel_spmd as _run

    nc = _bacc.Bacc("TRN2", target_bir_lowering=False, num_devices=1)
    arrays = {n: np.ascontiguousarray(inputs[n]) for n in _INS}
    arrays.update(_constants())
    d = {n: nc.dram_tensor(n, a.shape, mybir.dt.from_np(a.dtype), kind="ExternalInput").ap() for n, a in arrays.items()}
    out = nc.dram_tensor("out", [1, SEQ, D], F32, kind="ExternalOutput").ap()
    trunk(nc, d, out)
    r = _run(nc, [arrays], core_ids=[0])
    return r.results[0]["out"]
```

```python
import math
from contextlib import ExitStack

import numpy as np

import concourse.bass as bass
import concourse.mybir as mybir
from concourse.alu_op_type import AluOpType as ALU

F32 = mybir.dt.float32
I32 = mybir.dt.int32
F32R = mybir.dt.float32r
BF16 = mybir.dt.bfloat16
ACT = mybir.ActivationFunctionType
AX = mybir.AxisListType

P = 128
D, SEQ, DEPTH = 1024, 512, 2
NT = SEQ // P
KD = D // P
HD = 64
H_DIL, H_DSA, H_MLA = 6, 4, 6
DILATIONS = ((128, 1), (512, 4), (2048, 16))
H_IDX = 8
TOPK_KEYS = min(256, SEQ // 4)
RQ, RKV, NOPE, ROPE = 256, 128, 64, 32
MQ = NOPE + ROPE
N_BUCKETS, MAX_DISTANCE = 32, 2048
NE, TOPK, FF, SFF = 64, 8, 256, 256
ROUTED_SCALE = 2.5
ALPHA = (2 * DEPTH) ** 0.25
LN_EPS, RMS_EPS = 1e-5, 1e-6
SCALE = HD ** -0.5
MLA_SCALE = MQ ** -0.5
NEG = -1e30
TAKEN = -3e38
CAP = 100
MAX_PASSES = -(-SEQ // CAP)
ACC_ROWS = SEQ + P
NOT_ROUTED = 4096.0

C_DQ, C_DK, C_DV = 0, 384, 768
C_SQ, C_SK, C_SV = 1152, 1408, 1664
C_IQ, C_IK, C_IW = 1920, 2432, 2496
C_CQ, C_CKV, C_KR = 2504, 2760, 2888
IN_WIDTH = 2920
REST_WIDTH = IN_WIDTH - C_IW
CHUNKS = ((C_IW, REST_WIDTH // 2), (C_IW + REST_WIDTH // 2, REST_WIDTH // 2), (C_IK, HD), (C_IQ, 256), (C_IQ + 256, 256),
          (0, 256), (256, 256), (512, 256), (C_DV, 192), (C_DV + 192, 192),
          (C_SQ, 256), (C_SK, 256), (C_SV, 256))
CHUNK_MAX = 256
IK_CHUNK = 2
REST0 = C_IW
PEN_AT = {1: 0, 2: 2 * P, 3: 5 * P}
PEN_COLUMNS = 9 * P
SPAN = P + SEQ - 1


def _buckets(distance):
    exact = N_BUCKETS // 2
    d = np.maximum(distance, 1).astype(np.float64)
    large = exact + (np.log(d / exact) / math.log(MAX_DISTANCE / exact) * (N_BUCKETS - exact)).astype(np.int64)
    return np.where(distance < exact, distance, np.minimum(large, N_BUCKETS - 1))


def _constants():
    k = np.arange(SPAN + 1)
    dist = SEQ - 1 - k
    causal = dist >= 0
    onehot = ((_buckets(np.maximum(dist, 0))[None, :] == np.arange(N_BUCKETS)[:, None]) & causal)
    count = sum(((dist % d == 0) & (dist <= w)).astype(np.int64) for w, d in DILATIONS)
    logcount = np.where(causal & (count > 0), np.log(np.maximum(count, 1)), NEG)
    addend = np.concatenate([np.repeat(logcount[None], H_DIL, 0),
                             np.repeat(np.where(causal, 0.0, NEG)[None], H_DSA, 0)])
    p = np.arange(P)
    inv = 10000.0 ** (-np.arange(0, ROPE, 2) / ROPE)
    square = np.concatenate([np.eye(P), p[:, None] < p[None, :], np.ones((P, P))], 1)
    once = np.concatenate([np.eye(P)[::-1], np.repeat(np.arange(CAP)[None], P, 0)], 1)
    row = np.concatenate([np.repeat(inv[None], P, 0), (SEQ + p)[:, None],
                          p[:, None] + P * np.arange(NT)[None] - SEQ], 1)
    mask = np.where(p[:, None] + (SEQ - P) - np.arange(SEQ)[None] >= 0, 0.0, NEG)
    f = np.float32
    return {
        "c_square": square.astype(f),
        "c_once": once.astype(f),
        "c_row": row.astype(f),
        "c_mask": mask.astype(f),
        "c_onehot": onehot.astype(f),
        "c_addend": (addend / SCALE).astype(f),
    }


def _named(ctx, nc, names):
    return {n: ctx.enter_context(nc.semaphore(n)) for n in names.split()}


def _restart(nc, sems):
    numbers = [s.num for s in sems.values()]
    span = range(min(numbers), max(numbers) + 1)
    nc.gpsimd.dma_reset(span)
    nc.gpsimd.sem_clear(span)
    nc.all_engine_barrier()


def _setup(nc, d, sb):
    with ExitStack() as ctx:
        S = _named(ctx, nc, "consts_in x_in table_in positions_in bias_psum bias_row bias_row_out flip0_in flip1_in flip2_in flip3_in flip4_in mask_in bias_turned bias_out bias_stored "
                            "angle quarter sines zeros zeros_out numbers")
        raw = ctx.enter_context(nc.sbuf_tensor("raw_table", [N_BUCKETS, 10], F32))
        onehot = ctx.enter_context(nc.sbuf_tensor("onehot", [N_BUCKETS, SPAN + 1], F32))
        addend = ctx.enter_context(nc.sbuf_tensor("addend", [10, SPAN + 1], F32))
        brow = ctx.enter_context(nc.sbuf_tensor("brow", [10, SPAN + 1], F32))
        pos_i = ctx.enter_context(nc.sbuf_tensor("pos_i", [P, NT], I32))
        pos_f = ctx.enter_context(nc.sbuf_tensor("pos_f", [P, NT], F32))
        ang = ctx.enter_context(nc.sbuf_tensor("ang", [P, NT, 2, ROPE // 2], F32))
        turns = ctx.enter_context(nc.sbuf_tensor("turns", [P, NT, ROPE // 2], F32))
        turns_i = ctx.enter_context(nc.sbuf_tensor("turns_i", [P, NT, ROPE // 2], I32))
        zero = ctx.enter_context(nc.sbuf_tensor("zero", [P, D], F32))
        once = ctx.enter_context(nc.sbuf_tensor("once", [P, P + CAP], F32))
        bias = ctx.enter_context(nc.sbuf_tensor("bias_set", [P, 10, SEQ], F32))
        flipped = ctx.enter_context(nc.sbuf_tensor("flipped", [P, 10, SEQ], F32))
        ps = ctx.enter_context(nc.psum_tensor("ps_bias", [P, 2, 512], F32))
        ps_f = [ctx.enter_context(nc.psum_tensor(f"ps_flip{i}", [P, 512], F32)) for i in range(4)]
        half = (SPAN + 1) // 2
        x_in = d["x"].rearrange("o (t p) m -> p (o t) m", p=P)
        with nc.Block() as block:
            @block.sync
            def _(sp):
                sp.dma_start(raw[:], d["rel_bias"]).then_inc(S["table_in"], 16)
                sp.dma_start(onehot[:], d["c_onehot"]).then_inc(S["table_in"], 16)
                sp.dma_start(addend[:], d["c_addend"]).then_inc(S["table_in"], 16)
                sp.dma_start(sb["square"][:], d["c_square"]).then_inc(S["consts_in"], 16)
                sp.dma_start(once[:], d["c_once"]).then_inc(S["consts_in"], 16)
                sp.dma_start(pos_i[:], d["positions"].rearrange("o (t p) -> p (o t)", p=P), allow_slow_non_contiguous=True).then_inc(S["positions_in"], 16)
                sp.dma_start(sb["row"][:], d["c_row"]).then_inc(S["positions_in"], 16)
                sp.dma_start(sb["x"][:, 0:2], x_in[:, 0:2]).then_inc(S["x_in"], 16)
                sp.wait_ge(S["bias_row"], 2)
                sp.dma_start(d["bias_rows"], brow[:]).then_inc(S["bias_row_out"], 16)
                sp.wait_ge(S["zeros"], 1)
                sp.dma_start(d["x1_rows"][SEQ:ACC_ROWS, :], zero[:]).then_inc(S["zeros_out"], 16)
                sp.dma_start(d["acc_rows"][SEQ:ACC_ROWS, :], zero[:]).then_inc(S["zeros_out"], 16)
                sp.wait_ge(S["bias_row_out"], 16)
                for i in range(5):
                    sp.dma_start(flipped[:, 2 * i:2 * i + 2, :],
                                 bass.AP(d["bias_rows"].tensor, 2 * i * (SPAN + 1), [[1, P], [SPAN + 1, 2], [1, SEQ]])
                                 ).then_inc(S[f"flip{i}_in"], 16)
                sp.dma_start(sb["x"][:, 2:NT], x_in[:, 2:NT]).then_inc(S["x_in"], 16)
                sp.dma_start(sb["mask"][:], d["c_mask"]).then_inc(S["mask_in"], 16)
                for h in range(10):
                    sp.wait_ge(S["bias_out"], h + 1)
                    sp.dma_start(d["bias_tiles"][:, h, :], bias[:, h, :]).then_inc(S["bias_stored"], 16)
                sp.wait_ge(S["zeros_out"], 32)
                sp.wait_ge(S["bias_stored"], 160)
                sp.wait_ge(S["mask_in"], 16)
                sp.wait_ge(S["x_in"], 32)

            @block.tensor
            def _(pe):
                pe.wait_ge(S["table_in"], 48)
                for c in range(2):
                    pe.matmul(ps[0:10, c, 0:half], raw[:], onehot[:, c * half:(c + 1) * half],
                              start=True, stop=True).then_inc(S["bias_psum"], 1)
                pe.wait_ge(S["consts_in"], 32)
                for h in range(10):
                    if h % 2 == 0:
                        pe.wait_ge(S[f"flip{h // 2}_in"], 16)
                    if h >= 4:
                        pe.wait_ge(S["bias_out"], h - 3)
                    pe.matmul(ps_f[h % 4][:], once[:, 0:P], flipped[:, h, :], start=True, stop=True
                              ).then_inc(S["bias_turned"], 1)

            @block.vector
            def _(dve):
                dve.memset(zero[:], 0.0).then_inc(S["zeros"], 1)
                dve.wait_ge(S["table_in"], 48)
                for c in range(2):
                    dve.wait_ge(S["bias_psum"], c + 1)
                    dve.scalar_tensor_tensor(out=brow[:, c * half:(c + 1) * half], in0=ps[0:10, c, 0:half],
                                             scalar=1.0 / SCALE, in1=addend[:, c * half:(c + 1) * half],
                                             op0=ALU.mult, op1=ALU.add).then_inc(S["bias_row"], 1)
                dve.wait_ge(S["consts_in"], 32)
                dve.tensor_copy(sb["number"][:], once[:, P:P + CAP]).then_inc(S["numbers"], 1)
                dve.wait_ge(S["positions_in"], 32)
                dve.tensor_copy(pos_f[:], pos_i[:]).then_inc(S["angle"], 1)
                dve.wait_ge(S["angle"], 1)
                for t in range(NT):
                    dve.tensor_scalar(ang[:, t, 1, :], sb["row"][:, 0:ROPE // 2], pos_f[:, t:t + 1], None,
                                      ALU.mult).then_inc(S["angle"], 1)
                sines = ang[:, :, 1, :]
                steps = 1 + NT

                def done(i):
                    nonlocal steps
                    i.then_inc(S["angle"], 1)
                    steps += 1
                    dve.wait_ge(S["angle"], steps)

                dve.wait_ge(S["angle"], steps)
                done(dve.tensor_scalar(turns[:], sines, 1.0 / (2 * math.pi), None, ALU.mult))
                done(dve.tensor_copy(turns_i[:], turns[:]))
                done(dve.tensor_copy(turns[:], turns_i[:]))
                c1 = 6.28125
                c2 = float(np.float32(round((2 * math.pi - c1) * 2 ** 21) / 2 ** 21))
                c3 = 2 * math.pi - c1 - c2
                for part in (c1, c2, c3):
                    done(dve.scalar_tensor_tensor(out=sines, in0=turns[:], scalar=-part, in1=sines,
                                                  op0=ALU.mult, op1=ALU.add))
                done(dve.tensor_scalar(ang[:, :, 0, :], sines, math.pi / 2, None, ALU.add))
                done(dve.tensor_scalar(turns[:], ang[:, :, 0, :], math.pi, -2 * math.pi, ALU.is_gt, ALU.mult))
                done(dve.tensor_tensor(ang[:, :, 0, :], ang[:, :, 0, :], turns[:], ALU.add))
                lim = 3.1415925
                dve.tensor_scalar(ang[:], ang[:], lim, -lim, ALU.min, ALU.max).then_inc(S["quarter"], 1)

            @block.scalar
            def _(act):
                act.wait_ge(S["quarter"], 1)
                act.activation(sb["rope"][:], ang[:], ACT.Sin).then_inc(S["sines"], 1)
                for h in range(10):
                    act.wait_ge(S["bias_turned"], h + 1)
                    act.copy(bias[:, h, :], ps_f[h % 4][:]).then_inc(S["bias_out"], 1)
        _restart(nc, S)


def _units():
    u = [("xT", k) for k in range(KD)]
    u += [("rest", 0, t) for t in range(NT)] + [("rest", 1, t) for t in range(NT)]
    u += [("ik",)] + [("iq", m) for m in range(4)]
    u += [("cqT", j) for j in range(2)] + [("ckvT",)]
    u += [("idx", i, g) for i in (3, 2, 1) for g in range(H_IDX)]
    u += [("mq", t, c) for t in range(NT) for c in range(2)]
    u += [("dqk", m) for m in range(6)]
    u += [("kn", h) for h in range(H_MLA)] + [("mv", t) for t in range(NT)]
    u += [("qT", h) for h in range(H_MLA)] + [("krT",)]
    u += [("dv", c, t) for c in range(2) for t in range(NT)]
    u += [("sqk", m) for m in range(4)] + [("sv", t) for t in range(NT)]
    return u


BANKS1 = 8
LOWER_AT = {(3, 8): 7, (2, 0): 8, (2, 10): 9, (1, 6): 10}


def _projections(nc, d, sb, l):
    units = _units()
    place = {x: i for i, x in enumerate(units)}
    chunk_of = {"rest": lambda x: x[1], "ik": lambda x: IK_CHUNK, "iq": lambda x: 3 + x[1] // 2,
                "dqk": lambda x: 5 + x[1] // 2, "dv": lambda x: 8 + x[1], "sqk": lambda x: 10 + x[1] // 2,
                "sv": lambda x: 12}
    last_use = {chunk_of[x[0]](x): u for u, x in enumerate(units) if x[0] in chunk_of}
    split_after = {last_use[c - 2]: c for c in range(2, len(CHUNKS))}
    split_after[place[("rest", 0, 1)]] = 1
    with ExitStack() as ctx:
        S = _named(ctx, nc, "w_in w_hi w_lo xT_lo small_in unit_made unit_out rel_used "
                            "squares mean_squares root latent_ready dve_step q_roped k_roped pool_step kr_zero")
        wbuf = ctx.enter_context(nc.sbuf_tensor("wbuf", [P, KD, CHUNK_MAX], F32))
        w_hi = ctx.enter_context(nc.sbuf_tensor("w_hi", [P, 2, KD, CHUNK_MAX], F32R))
        w_lo = ctx.enter_context(nc.sbuf_tensor("w_lo", [P, 2, KD, CHUNK_MAX], F32R))
        xT_hi = ctx.enter_context(nc.sbuf_tensor("xT_hi", [P, KD, SEQ], F32R))
        xT_lo = ctx.enter_context(nc.sbuf_tensor("xT_lo", [P, KD, SEQ], F32R))
        w_uq = ctx.enter_context(nc.sbuf_tensor("w_uq", [P, 2, H_MLA * MQ], F32))
        w_ukv = ctx.enter_context(nc.sbuf_tensor("w_ukv", [P, H_MLA, 2, HD], F32))
        g_q = ctx.enter_context(nc.sbuf_tensor("g_q", [P, 2], F32))
        g_kv = ctx.enter_context(nc.sbuf_tensor("g_kv", [P, 1], F32))
        ikT = ctx.enter_context(nc.sbuf_tensor("ikT", [P, SEQ], F32))
        rest = ctx.enter_context(nc.sbuf_tensor("rest", [P, NT, IN_WIDTH - REST0], F32))
        cqT = ctx.enter_context(nc.sbuf_tensor("cqT", [P, 2, SEQ], F32))
        ckvT = ctx.enter_context(nc.sbuf_tensor("ckvT", [P, SEQ], F32))
        q_tm = ctx.enter_context(nc.sbuf_tensor("q_tm", [P, NT, H_MLA, MQ], F32))
        iqT = q_tm[:].rearrange("p t h c -> p (t h c)")[:, 0:4 * SEQ].rearrange("p (m s) -> p m s", m=4)
        rot = ctx.enter_context(nc.sbuf_tensor("rot", [P, 2, NT, H_MLA, ROPE // 2], F32))
        kr = ctx.enter_context(nc.sbuf_tensor("kr", [P, NT, MQ], F32))
        rel = ctx.enter_context(nc.sbuf_tensor("rel", [P, 2, SEQ], F32))
        score = ctx.enter_context(nc.sbuf_tensor("score", [P, PEN_COLUMNS], F32))
        top8 = ctx.enter_context(nc.sbuf_tensor("top8", [P, 8], F32))
        ms = ctx.enter_context(nc.sbuf_tensor("ms", [P, 2, NT], F32))
        ps = [ctx.enter_context(nc.psum_tensor(f"pp{i}", [P, 512], F32)) for i in range(BANKS1)]
        x_sb = sb["x"]
        junk = score
        ident = sb["square"][:, 0:P]
        iw = lambda i, g: rest[:, i, g:g + 1]
        cq = rest[:, :, C_CQ - REST0:C_CKV - REST0]
        ckv = rest[:, :, C_CKV - REST0:C_KR - REST0]
        kraw = rest[:, :, C_KR - REST0:IN_WIDTH - REST0]
        cos, sin = sb["rope"][:, :, 0, :], sb["rope"][:, :, 1, :]

        with nc.Block() as block:
            @block.sync
            def _(sp):
                w = d["w_in"][bass.ds(l, 1)].rearrange("o (p k) c -> p (o k) c", k=KD)

                def chunk(c):
                    if c:
                        sp.wait_ge(S["w_lo"], c)
                    c0, n = CHUNKS[c]
                    sp.dma_start(wbuf[:, :, 0:n], w[:, :, c0:c0 + n]).then_inc(S["w_in"], 16)

                chunk(0)
                sp.dma_start(g_q[:], d["mla_q_norm"][bass.ds(l, 1)].rearrange("o (j p) -> p (o j)", p=P), allow_slow_non_contiguous=True).then_inc(S["small_in"], 16)
                sp.dma_start(g_kv[:], d["mla_kv_norm"][bass.ds(l, 1)].rearrange("o (j p) -> p (o j)", p=P), allow_slow_non_contiguous=True).then_inc(S["small_in"], 16)
                sp.dma_start(w_uq[:], d["mla_w_uq"][bass.ds(l, 1)].rearrange("o (j p) c -> p (o j) c", p=P)).then_inc(S["small_in"], 16)
                sp.dma_start(w_ukv[:].rearrange("p h a c -> p (h a c)"),
                             d["mla_w_ukv"][bass.ds(l, 1)].rearrange("o p c -> p (o c)")).then_inc(S["small_in"], 16)
                for c in range(1, len(CHUNKS)):
                    chunk(c)

            @block.tensor
            def _(pe):
                waited = set()
                for u, x in enumerate(units):
                    kind = x[0]
                    out = ps[u % BANKS1]
                    if u >= BANKS1:
                        pe.wait_ge(S["unit_out"], u - BANKS1 + 1)
                    if kind in chunk_of and chunk_of[kind](x) not in waited:
                        c = chunk_of[kind](x)
                        waited.add(c)
                        pe.wait_ge(S["w_lo"], c + 1)
                        wc_hi, wc_lo = w_hi[:, c % 2], w_lo[:, c % 2]
                    if x == ("rest", 0, 0):
                        pe.wait_ge(S["unit_out"], KD)
                        pe.wait_ge(S["xT_lo"], KD)
                    if kind == "xT":
                        for t in range(NT):
                            mm = pe.transpose(out[:, t * P:(t + 1) * P], x_sb[:, t, x[1]::KD], ident)
                    elif kind in ("rest", "dv", "sv"):
                        t = x[-1]
                        n = CHUNKS[c][1]
                        rows = slice(t * P, (t + 1) * P)
                        for k in range(KD):
                            pe.matmul(out[:, 0:n], xT_hi[:, k, rows], wc_hi[:, k, 0:n], start=(k == 0), stop=False)
                            pe.matmul(out[:, 0:n], xT_hi[:, k, rows], wc_lo[:, k, 0:n], start=False, stop=False)
                            mm = pe.matmul(out[:, 0:n], xT_lo[:, k, rows], wc_hi[:, k, 0:n],
                                           start=False, stop=(k == KD - 1))
                    elif kind in ("ik", "iq", "dqk", "sqk"):
                        m = x[1] % 2 if kind != "ik" else 0
                        cols = slice(m * P, (m + 1) * P)
                        for k in range(KD):
                            pe.matmul(out[:, :], wc_hi[:, k, cols], xT_hi[:, k, :], start=(k == 0), stop=False)
                            pe.matmul(out[:, :], wc_hi[:, k, cols], xT_lo[:, k, :], start=False, stop=False)
                            mm = pe.matmul(out[:, :], wc_lo[:, k, cols], xT_hi[:, k, :],
                                           start=False, stop=(k == KD - 1))
                    elif kind in ("cqT", "ckvT"):
                        if x == ("cqT", 0):
                            pe.wait_ge(S["latent_ready"], 2 * NT)
                        for t in range(NT):
                            src = cq[:, t, x[1] * P:(x[1] + 1) * P] if kind == "cqT" else ckv[:, t, :]
                            mm = pe.transpose(out[:, t * P:(t + 1) * P], src, ident)
                    elif kind == "idx":
                        i, g = x[1:]
                        if x == ("idx", 3, 0):
                            pe.wait_ge(S["unit_out"], place[("iq", 3)] + 1)
                        a = HD * (g % 2)
                        mm = pe.matmul(out[:, 0:P * (i + 1)], iqT[a:a + HD, g // 2, i * P:(i + 1) * P],
                                       ikT[a:a + HD, 0:P * (i + 1)], start=True, stop=True)
                    elif kind == "mq":
                        t, c2 = x[1:]
                        if x == ("mq", 0, 0):
                            pe.wait_ge(S["unit_out"], place[("ckvT",)] + 1)
                            pe.wait_ge(S["small_in"], 64)
                        n = H_MLA * MQ // 2
                        for j in range(2):
                            mm = pe.matmul(out[:, 0:n], cqT[:, j, t * P:(t + 1) * P],
                                           w_uq[:, j, c2 * n:(c2 + 1) * n], start=(j == 0), stop=(j == 1))
                    elif kind == "kn":
                        mm = pe.matmul(out[0:HD, :], w_ukv[:, x[1], 0, :], ckvT[:, :], start=True, stop=True)
                    elif kind == "mv":
                        mm = pe.matmul(out[:, 0:H_MLA * HD].rearrange("p (h c) -> p h c", c=HD),
                                       ckvT[:, x[1] * P:(x[1] + 1) * P], w_ukv[:, :, 1, :],
                                       start=True, stop=True)
                    elif kind == "qT":
                        if x[1] == 0:
                            pe.wait_ge(S["q_roped"], 2)
                        for t in range(NT):
                            mm = pe.transpose(out[0:MQ, t * P:(t + 1) * P], q_tm[:, t, x[1], :], ident)
                    elif kind == "krT":
                        pe.wait_ge(S["k_roped"], 2)
                        pe.wait_ge(S["kr_zero"], 1)
                        for t in range(NT):
                            mm = pe.transpose(out[0:MQ, t * P:(t + 1) * P], kr[:, t, :], ident)
                    mm.then_inc(S["unit_made"], 1)

            def halves(c):
                n = CHUNKS[c][1]
                if c == IK_CHUNK:
                    twice = lambda w: w[:, c % 2, :, 0:2 * n].rearrange("p k (a c) -> p k a c", a=2)
                    return wbuf[:, :, 0:n].unsqueeze(2).to_broadcast([P, KD, 2, n]), twice(w_hi), twice(w_lo)
                return wbuf[:, :, 0:n], w_hi[:, c % 2, :, 0:n], w_lo[:, c % 2, :, 0:n]

            @block.scalar
            def _(act):
                def upper(c):
                    act.wait_ge(S["w_in"], 16 * (c + 1))
                    if c >= 2:
                        act.wait_ge(S["unit_made"], last_use[c - 2] + 1)
                    raw, hi, lo = halves(c)
                    act.copy(hi, raw).then_inc(S["w_hi"], 1)

                for u, x in enumerate(units):
                    kind = x[0]
                    src = ps[u % BANKS1]
                    act.wait_ge(S["unit_made"], u + 1)
                    if kind == "xT":
                        o = act.copy(xT_hi[:, x[1], :], src[:, :])
                    elif kind == "rest":
                        c0, n = CHUNKS[x[1]]
                        o = act.copy(rest[:, x[2], c0 - REST0:c0 - REST0 + n], src[:, 0:n])
                    elif kind == "ik":
                        o = act.copy(ikT[:, :], src[:, :])
                    elif kind == "iq":
                        o = act.copy(iqT[:, x[1], :], src[:, :])
                    elif kind == "cqT":
                        if x[1] == 0:
                            act.wait_ge(S["small_in"], 64)
                        o = act.activation(cqT[:, x[1], :], src[:, :], ACT.Copy, scale=g_q[:, x[1]:x[1] + 1])
                    elif kind == "ckvT":
                        o = act.activation(ckvT[:, :], src[:, :], ACT.Copy, scale=g_kv[:, 0:1])
                    elif kind == "idx":
                        n = u - place[("idx", 3, 0)]
                        if n >= 2:
                            act.wait_ge(S["rel_used"], n - 1)
                        w = P * (x[1] + 1)
                        o = act.activation(rel[:, n % 2, 0:w], src[:, 0:w], ACT.Relu)
                    elif kind == "mq":
                        hh = H_MLA // 2
                        o = act.copy(q_tm[:, x[1], x[2] * hh:(x[2] + 1) * hh, :].rearrange("p h c -> p (h c)"),
                                     src[:, 0:hh * MQ])
                    elif kind == "kn":
                        o = act.copy(sb["mkT"][0:HD, x[1], :], src[0:HD, :])
                    elif kind == "mv":
                        o = act.copy(sb["mv"][:, x[1], :], src[:, 0:H_MLA * HD])
                    elif kind == "qT":
                        o = act.copy(sb["mqT"][0:MQ, x[1], :], src[0:MQ, :])
                    elif kind == "krT":
                        o = act.copy(sb["mkT"][HD:MQ, :, :],
                                     src[HD:MQ, :].unsqueeze(1).to_broadcast([ROPE, H_MLA, SEQ]))
                    elif kind == "dqk":
                        o = act.copy(sb["dqkT"][:, x[1], :], src[:, :])
                    elif kind == "dv":
                        o = act.copy(sb["dv"][:, x[2], x[1] * 192:x[1] * 192 + 192], src[:, 0:192])
                    elif kind == "sqk":
                        o = act.copy(sb["sqkT"][:, x[1], :], src[:, :])
                    elif kind == "sv":
                        o = act.copy(sb["sv"][:, x[1], :], src[:, 0:256])
                    o.then_inc(S["unit_out"], 1)
                    if x == ("xT", KD - 1):
                        upper(0)
                    if u in split_after:
                        upper(split_after[u])
                    if x == ("rest", 1, NT - 1):
                        act.wait_ge(S["unit_out"], u + 1)
                        for t in range(NT):
                            if t:
                                act.wait_ge(S["squares"], 2 * t)
                            act.activation(junk[:, 0:RQ], cq[:, t, :], ACT.Square,
                                           accum_out=ms[:, 0, t:t + 1]).then_inc(S["squares"], 1)
                            act.wait_ge(S["squares"], 2 * t + 1)
                            act.activation(junk[:, 0:RKV], ckv[:, t, :], ACT.Square,
                                           accum_out=ms[:, 1, t:t + 1]).then_inc(S["squares"], 1)
                        act.wait_ge(S["mean_squares"], 2)
                        act.activation(ms[:], ms[:], ACT.Sqrt).then_inc(S["root"], 1)

            @block.vector
            def _(dve):
                steps = 0

                def step(i):
                    nonlocal steps
                    i.then_inc(S["dve_step"], 1)
                    steps += 1
                    dve.wait_ge(S["dve_step"], steps)

                def lower(c):
                    dve.wait_ge(S["w_hi"], c + 1)
                    raw, hi, lo = halves(c)
                    dve.tensor_tensor(lo, raw, hi.bitcast(F32), ALU.subtract).then_inc(S["w_lo"], 1)

                dve.memset(kr[:, :, 0:HD], 0.0).then_inc(S["kr_zero"], 1)
                for k in range(KD):
                    dve.wait_ge(S["unit_out"], k + 1)
                    dve.tensor_tensor(xT_lo[:, k, :], ps[k][:], xT_hi[:, k, :].bitcast(F32), ALU.subtract
                                      ).then_inc(S["xT_lo"], 1)
                for c in range(4):
                    lower(c)
                dve.wait_ge(S["squares"], 2 * NT)
                for j, n in enumerate((RQ, RKV)):
                    dve.tensor_scalar(ms[:, j, :], ms[:, j, :], 1.0 / n, RMS_EPS, ALU.mult, ALU.add
                                      ).then_inc(S["mean_squares"], 1)
                dve.wait_ge(S["root"], 1)
                step(dve.reciprocal(ms[:], ms[:]))
                for t in range(NT):
                    dve.tensor_scalar(cq[:, t, :], cq[:, t, :], ms[:, 0, t:t + 1], None, ALU.mult
                                      ).then_inc(S["latent_ready"], 1)
                    dve.tensor_scalar(ckv[:, t, :], ckv[:, t, :], ms[:, 1, t:t + 1], None, ALU.mult
                                      ).then_inc(S["latent_ready"], 1)
                for c in range(4, 7):
                    lower(c)
                n = 0
                for i in (3, 2, 1):
                    w = P * (i + 1)
                    sc = score[:, PEN_AT[i]:PEN_AT[i] + w]
                    for g in range(H_IDX):
                        dve.wait_ge(S["unit_out"], place[("idx", i, g)] + 1)
                        if g == 0:
                            o = dve.tensor_scalar(sc, rel[:, n % 2, 0:w], iw(i, g), None, ALU.mult)
                        else:
                            dve.wait_ge(S["rel_used"], n)
                            o = dve.scalar_tensor_tensor(out=sc, in0=rel[:, n % 2, 0:w], scalar=iw(i, g),
                                                         in1=sc, op0=ALU.mult, op1=ALU.add)
                        o.then_inc(S["rel_used"], 1)
                        n += 1
                    dve.wait_ge(S["rel_used"], n)
                    diag = score[:, PEN_AT[i] + w - P:PEN_AT[i] + w]
                    step(dve.tensor_tensor(diag, diag, sb["mask"][:, SEQ - P:SEQ], ALU.add))
                for i in (3, 2, 1):
                    w = P * (i + 1)
                    sc = score[:, PEN_AT[i]:PEN_AT[i] + w]
                    for q in range(TOPK_KEYS // 8):
                        if (i, q) in LOWER_AT:
                            lower(LOWER_AT[i, q])
                        step(dve.max(top8[:], sc))
                        step(dve.match_replace(sc, top8[:], sc, TAKEN))
                    dve.tensor_scalar(sb["pen"][:, PEN_AT[i]:PEN_AT[i] + w], sc, TAKEN / 2, NEG, ALU.is_gt, ALU.mult)
                for c in range(11, len(CHUNKS)):
                    lower(c)

            @block.gpsimd
            def _(pool):
                steps = 0

                def step(i):
                    nonlocal steps
                    i.then_inc(S["pool_step"], 1)
                    steps += 1
                    pool.wait_ge(S["pool_step"], steps)

                half = ROPE // 2

                def rope(lo, hi, out_lo, out_hi, c, s, r, done):
                    step(pool.tensor_tensor(r[0], lo, s, ALU.mult))
                    step(pool.tensor_tensor(r[1], hi, s, ALU.mult))
                    step(pool.tensor_tensor(out_lo, lo, c, ALU.mult))
                    step(pool.tensor_tensor(out_hi, hi, c, ALU.mult))
                    pool.tensor_tensor(out_lo, out_lo, r[1], ALU.subtract).then_inc(done, 1)
                    pool.tensor_tensor(out_hi, out_hi, r[0], ALU.add).then_inc(done, 1)

                pool.wait_ge(S["unit_out"], place[("rest", 1, NT - 1)] + 1)
                rope(kraw[:, :, 0:half], kraw[:, :, half:ROPE], kr[:, :, HD:HD + half], kr[:, :, HD + half:MQ],
                     cos, sin, [rot[:, j, :, 0, :] for j in range(2)], S["k_roped"])
                pool.wait_ge(S["unit_out"], place[("mq", NT - 1, 1)] + 1)
                bc = lambda a: a.unsqueeze(2).to_broadcast([P, NT, H_MLA, half])
                lo, hi = q_tm[:, :, :, NOPE:NOPE + half], q_tm[:, :, :, NOPE + half:MQ]
                pool.wait_ge(S["k_roped"], 2)
                rope(lo, hi, lo, hi, bc(cos), bc(sin), [rot[:, j] for j in range(2)], S["q_roped"])
        _restart(nc, S)


def _attention(nc, d, sb, l):
    heads = ([("mla", h) for h in range(H_MLA)] + [("dil", h) for h in range(H_DIL)]
             + [("dsa", h) for h in range(H_DSA)])
    column = {"dil": 0, "dsa": H_DIL, "mla": H_DIL + H_DSA}
    units = [(kind, h, i) for kind, h in heads for i in range(NT)]
    NU = len(units)
    NS, NP, NTB = 3, 3, 2
    with ExitStack() as ctx:
        S = _named(ctx, nc, "scores_made logits_out probs_out turned probsT_out heads_made head_out "
                            "pen_added recips w_out_in bias_in")
        bias = ctx.enter_context(nc.sbuf_tensor("bias", [P, 10, SEQ], F32))
        neg = ctx.enter_context(nc.sbuf_tensor("neg_logits", [P, NS, SEQ], F32))
        probs = ctx.enter_context(nc.sbuf_tensor("probs", [P, NP, SEQ], F32))
        probsT = ctx.enter_context(nc.sbuf_tensor("probsT", [P, NTB, SEQ], F32))
        negmax = ctx.enter_context(nc.sbuf_tensor("negmax", [P, NU], F32))
        total = ctx.enter_context(nc.sbuf_tensor("total", [P, NU], F32))
        recip = ctx.enter_context(nc.sbuf_tensor("recip", [P, NU], F32))
        dsa_bias = ctx.enter_context(nc.sbuf_tensor("dsa_bias", [P, H_DSA, PEN_COLUMNS], F32))
        ps_s = [ctx.enter_context(nc.psum_tensor(f"ps_s{i}", [P, 512], F32)) for i in range(NS)]
        ps_t = [ctx.enter_context(nc.psum_tensor(f"ps_t{i}", [P, 512], F32)) for i in range(NTB)]
        ps_o = [ctx.enter_context(nc.psum_tensor(f"ps_o{i}", [P, NT, P], F32)) for i in range(2)]
        ident = sb["square"][:, 0:P]
        o_sb = sb["o"]
        at = PEN_AT

        def q_of(kind, h, i):
            cols = slice(i * P, (i + 1) * P)
            a = HD * (h % 2)
            if kind == "dil":
                return sb["dqkT"][a:a + HD, h // 2, cols]
            if kind == "dsa":
                return sb["sqkT"][a:a + HD, h // 2, cols]
            return sb["mqT"][0:MQ, h, cols]

        def k_of(kind, h, w):
            a = HD * (h % 2)
            if kind == "dil":
                return sb["dqkT"][a:a + HD, H_DIL // 2 + h // 2, 0:w]
            if kind == "dsa":
                return sb["sqkT"][a:a + HD, H_DSA // 2 + h // 2, 0:w]
            return sb["mkT"][0:MQ, h, 0:w]

        def v_of(kind, h, j):
            return sb[{"dil": "dv", "dsa": "sv", "mla": "mv"}[kind]][:, j, h * HD:(h + 1) * HD]

        def bias_of(kind, h, i):
            w = P * (i + 1)
            if kind == "mla":
                return sb["mask"][:, SEQ - w:SEQ]
            if kind == "dil" or i == 0:
                return bias[:, h + (H_DIL if kind == "dsa" else 0), SEQ - w:SEQ]
            return dsa_bias[:, h, at[i]:at[i] + w]

        with nc.Block() as block:
            @block.sync
            def _(sp):
                sp.dma_start(bias[:], d["bias_tiles"]).then_inc(S["bias_in"], 16)
                sp.dma_start(sb["w_out"][:], d["w_out"][bass.ds(l, 1)].rearrange("o (p k) c -> p (o k) c", k=KD)
                             ).then_inc(S["w_out_in"], 16)
                sp.wait_ge(S["w_out_in"], 16)

            @block.tensor
            def _(pe):
                def scores(u):
                    kind, h, i = units[u]
                    w = P * (i + 1)
                    if u >= NS:
                        pe.wait_ge(S["logits_out"], u - NS + 1)
                    pe.matmul(ps_s[u % NS][:, 0:w], q_of(kind, h, i), k_of(kind, h, w),
                              start=True, stop=True).then_inc(S["scores_made"], 1)

                def turn(u):
                    kind, h, i = units[u]
                    pe.wait_ge(S["probs_out"], u + 1)
                    for j in range(i + 1):
                        mm = pe.transpose(ps_t[u % NTB][:, j * P:(j + 1) * P], probs[:, u % NP, j * P:(j + 1) * P], ident)
                    mm.then_inc(S["turned"], 1)

                def values(u):
                    kind, h, i = units[u]
                    pe.wait_ge(S["probsT_out"], u + 1)
                    n = u // NT
                    if i == 0 and n >= 2:
                        pe.wait_ge(S["head_out"], n - 1)
                    for j in range(i + 1):
                        mm = pe.matmul(ps_o[n % 2][:, i, 0:HD], probsT[:, u % NTB, j * P:(j + 1) * P],
                                       v_of(kind, h, j), start=(j == 0), stop=(j == i))
                    mm.then_inc(S["heads_made"], 1)

                scores(0)
                scores(1)
                for u in range(NU):
                    if u + 2 < NU:
                        scores(u + 2)
                    turn(u)
                    if u >= 1:
                        values(u - 1)
                values(NU - 1)

            @block.vector
            def _(dve):
                def head_out(n):
                    kind, h = heads[n]
                    dve.wait_ge(S["probs_out"], NT * (n + 1))
                    dve.reciprocal(recip[:, NT * n:NT * n + NT], total[:, NT * n:NT * n + NT]).then_inc(S["recips"], 1)
                    dve.wait_ge(S["recips"], n + 1)
                    dve.wait_ge(S["heads_made"], NT * (n + 1))
                    c = (column[kind] + h) * HD
                    dve.tensor_tensor(o_sb[:, :, c:c + HD], ps_o[n % 2][:, :, 0:HD],
                                      recip[:, NT * n:NT * n + NT].unsqueeze(2).to_broadcast([P, NT, HD]),
                                      ALU.mult).then_inc(S["head_out"], 1)

                for u, (kind, h, i) in enumerate(units):
                    w = P * (i + 1)
                    dve.wait_ge(S["scores_made"], u + 1)
                    if u >= NS:
                        dve.wait_ge(S["probs_out"], u - NS + 1)
                    if kind == "dil" and h == 0 and i == 0:
                        dve.wait_ge(S["bias_in"], 16)
                    if kind == "dsa" and i:
                        dve.wait_ge(S["pen_added"], 3 * h + i)
                    dve.tensor_tensor_reduce(neg[:, u % NS, 0:w], ps_s[u % NS][:, 0:w], bias_of(kind, h, i),
                                             -(MLA_SCALE if kind == "mla" else SCALE), 3e38, ALU.add, ALU.min,
                                             negmax[:, u:u + 1]).then_inc(S["logits_out"], 1)
                    if i == 2 and u > NT:
                        head_out(u // NT - 1)
                head_out(len(heads) - 1)

            @block.scalar
            def _(act):
                def probs_t(u):
                    w = P * (units[u][2] + 1)
                    act.wait_ge(S["turned"], u + 1)
                    if u >= NTB:
                        act.wait_ge(S["heads_made"], u - NTB + 1)
                    act.copy(probsT[:, u % NTB, 0:w], ps_t[u % NTB][:, 0:w]).then_inc(S["probsT_out"], 1)

                for u, (kind, h, i) in enumerate(units):
                    w = P * (i + 1)
                    act.wait_ge(S["logits_out"], u + 1)
                    if u >= NP:
                        act.wait_ge(S["turned"], u - NP + 1)
                    act.activation(probs[:, u % NP, 0:w], neg[:, u % NS, 0:w], ACT.Exp, bias=negmax[:, u:u + 1],
                                   scale=-1.0, accum_out=total[:, u:u + 1]).then_inc(S["probs_out"], 1)
                    if u >= 1:
                        probs_t(u - 1)
                probs_t(NU - 1)

            @block.gpsimd
            def _(pool):
                pool.wait_ge(S["bias_in"], 16)
                for h in range(H_DSA):
                    for i in range(1, NT):
                        w = P * (i + 1)
                        pool.tensor_tensor(dsa_bias[:, h, at[i]:at[i] + w], bias[:, H_DIL + h, SEQ - w:SEQ],
                                           sb["pen"][:, PEN_AT[i]:PEN_AT[i] + w], ALU.add).then_inc(S["pen_added"], 1)
        _restart(nc, S)


NORM_SEMS = "row_sum mean variance variance_eps deviation inverse centred"


def _norm_squares(act, S, r, st, junk, t):
    act.wait_ge(S["mean"], t + 1)
    act.activation(junk[:], r, ACT.Square, bias=st[:, 1, t:t + 1], accum_out=st[:, 2, t:t + 1]).then_inc(S["variance"], 1)


def _norm_deviation(act, S, st, t):
    act.wait_ge(S["variance_eps"], t + 1)
    act.activation(st[:, 3, t:t + 1], st[:, 3, t:t + 1], ACT.Sqrt).then_inc(S["deviation"], 1)


def _norm_mean(dve, S, st, t):
    dve.wait_ge(S["row_sum"], t + 1)
    dve.tensor_scalar(st[:, 1, t:t + 1], st[:, 0, t:t + 1], -1.0 / D, None, ALU.mult).then_inc(S["mean"], 1)


def _norm_centre(dve, S, r, st, gain, out, t):
    dve.wait_ge(S["mean"], t + 1)
    dve.scalar_tensor_tensor(out=out, in0=r, scalar=st[:, 1, t:t + 1], in1=gain[:], op0=ALU.add, op1=ALU.mult
                             ).then_inc(S["centred"], 1)


def _norm_variance(dve, S, st, t):
    dve.wait_ge(S["variance"], t + 1)
    dve.tensor_scalar(st[:, 3, t:t + 1], st[:, 2, t:t + 1], 1.0 / D, LN_EPS, ALU.mult, ALU.add).then_inc(S["variance_eps"], 1)


def _norm_scale(dve, S, st, shift, out, t, done):
    dve.wait_ge(S["deviation"], t + 1)
    dve.reciprocal(st[:, 4, t:t + 1], st[:, 3, t:t + 1]).then_inc(S["inverse"], 1)
    dve.wait_ge(S["inverse"], t + 1)
    dve.wait_ge(S["centred"], t + 1)
    dve.scalar_tensor_tensor(out=out, in0=out, scalar=st[:, 4, t:t + 1], in1=shift[:], op0=ALU.mult, op1=ALU.add
                             ).then_inc(done, 1)


def _place_parts(dve, step, sb):
    step(dve.tensor_copy(sb["parts"][:, 0, :, :, 0], sb["placed"][:]))
    step(dve.tensor_tensor(sb["parts"][:, 1, :, :, 0], sb["placed"][:], sb["parts"][:, 0, :, :, 0], ALU.subtract))


def _mix_and_route(nc, d, sb, l):
    with ExitStack() as ctx:
        S = _named(ctx, nc, NORM_SEMS + " norm_in small_in shared_in oT_made oT_out mixed mix_read x1_ready x1_out x1T_made x1T_out "
                            "logits_made exps up_made silu_out gated down_made acc_ready acc0_out acc1_out "
                            "ahead_in mask_ready pos_made pos_read route_step  tables")
        T = lambda name, shape, dt=F32: ctx.enter_context(nc.sbuf_tensor(name, shape, dt))
        oT = T("oT", [P, 2, KD, P])
        r = T("r", [P, 2, D])
        junk = T("junk3", [P, D])
        st = T("st3", [P, 5, NT])
        gain, shift = T("gain1", [P, D]), T("shift1", [P, D])
        x1T = T("x1T", [P, KD, SEQ])
        rw = T("rw", [P, KD, NE])
        rb = T("rb", [P, NE])
        w13 = T("sh_w13", [P, 2, KD, SFF])
        w2 = T("sh_w2_sb", [P, 2, D])
        act_out = T("sh_silu", [P, 2, SEQ])
        shT = T("shT", [P, 2, SEQ])
        acc = T("acc_sb", [P, 2, D])
        e, s, sel, left, mask, gate = (T(n, [P, NT, NE]) for n in ("e", "s", "sel", "left", "picked", "gate_raw"))
        top8 = T("top8r", [P, NT, 8])
        gsum = T("gsum", [P, 2, NT])
        cnt = T("cnt", [P, MAX_PASSES])
        ps = lambda name, shape: ctx.enter_context(nc.psum_tensor(name, shape, F32))
        ps_a, ps_mix, ps_x = ps("ps_a", [P, KD, P]), ps("ps_mix", [P, D]), ps("ps_x", [P, KD, P])
        ps_r, ps_c = ps("ps_r", [P, 2, NT, NE]), ps("ps_c", [P, 512])
        flat_a, flat_x = (q[:].rearrange("p k c -> p (k c)") for q in (ps_a, ps_x))
        early = SEQ - P
        square = sb["square"]
        ident, earlier, ones = square[:, 0:P], square[:, P:2 * P], square[:, 2 * P:3 * P]
        x_sb, o_sb = sb["x"], sb["o"]
        up_bank = [flat_a[:, 0:512], flat_a[:, 512:1024], ps_mix[:, 0:512], ps_mix[:, 512:1024]]
        dn_bank = [flat_x, flat_a]

        with nc.Block() as block:
            @block.sync
            def _(sp):
                row = lambda name, n: d[name][bass.ds(l, 1)].to_broadcast([P, n])
                sp.dma_start(gain[:], row("ln1_g", D)).then_inc(S["norm_in"], 16)
                sp.dma_start(shift[:], row("ln1_b", D)).then_inc(S["norm_in"], 16)
                sp.dma_start(rb[:], row("router_bias", NE)).then_inc(S["small_in"], 16)
                sp.dma_start(rw[:], d["router_w"][bass.ds(l, 1)].rearrange("o (p k) e -> p (o k) e", k=KD)).then_inc(S["small_in"], 16)
                for j, name in enumerate(("sh_w1", "sh_w3")):
                    sp.dma_start(w13[:, j], d[name][bass.ds(l, 1)].rearrange("o (p k) f -> p (o k) f", k=KD)).then_inc(S["shared_in"], 16)
                sp.dma_start(w2[:], d["sh_w2"][bass.ds(l, 1)].rearrange("o (m p) c -> p (o m) c", p=P)).then_inc(S["shared_in"], 16)
                _load_ahead(sp, d, sb, l, S["ahead_in"])
                for t in range(NT):
                    sp.wait_ge(S["x1_ready"], t + 1)
                    sp.dma_start(d["x1_rows"][t * P:(t + 1) * P, :], x_sb[:, t, :]).then_inc(S["x1_out"], 16)
                for t in range(NT):
                    sp.wait_ge(S["acc_ready"], t + 1)
                    sp.dma_start(d["acc_rows"][t * P:(t + 1) * P, :], acc[:, t % 2, :]).then_inc(S[f"acc{t % 2}_out"], 16)
                sp.wait_ge(S["x1_out"], 64)
                sp.wait_ge(S["ahead_in"], AHEAD)
                for b in range(2):
                    sp.wait_ge(S[f"acc{b}_out"], 32)

            @block.tensor
            def _(pe):
                def turn_o(t):
                    if t:
                        pe.wait_ge(S["oT_out"], t)
                    for k in range(KD):
                        mm = pe.transpose(ps_a[:, k, :], o_sb[:, t, k::KD], ident)
                    mm.then_inc(S["oT_made"], 1)

                def mix(t):
                    pe.wait_ge(S["oT_out"], t + 1)
                    if t:
                        pe.wait_ge(S["row_sum"], t)
                    for c in range(2):
                        for k in range(KD):
                            mm = pe.matmul(ps_mix[:, c * 512:(c + 1) * 512], oT[:, t % 2, k, :],
                                           sb["w_out"][:, k, c * 512:(c + 1) * 512], start=(k == 0), stop=(k == KD - 1))
                    mm.then_inc(S["mixed"], 1)

                def turn_x(t):
                    pe.wait_ge(S["x1_ready"], t + 1)
                    if t:
                        pe.wait_ge(S["x1T_out"], t)
                    for k in range(KD):
                        mm = pe.transpose(ps_x[:, k, :], x_sb[:, t, k::KD], ident)
                    mm.then_inc(S["x1T_made"], 1)

                def router(t):
                    pe.wait_ge(S["x1T_out"], t + 1)
                    pe.wait_ge(S["small_in"], 32)
                    for k in range(KD):
                        mm = pe.matmul(ps_r[:, 0, t, :], x1T[:, k, t * P:(t + 1) * P], rw[:, k, :],
                                       start=(k == 0), stop=(k == KD - 1))
                    mm.then_inc(S["logits_made"], 1)

                def shared_up(q, first, last):
                    for k in range(KD):
                        mm = pe.matmul(up_bank[q][:, first:last], w13[:, q // 2, k, (q % 2) * P:(q % 2 + 1) * P],
                                       x1T[:, k, first:last], start=(k == 0), stop=(k == KD - 1))
                    return mm

                turn_o(0)
                turn_o(1)
                for t in range(NT):
                    mix(t)
                    if t + 2 < NT:
                        turn_o(t + 2)
                    if t >= 1:
                        turn_x(t - 1)
                    if t >= 2:
                        router(t - 2)
                pe.wait_ge(S["shared_in"], 48)
                pe.wait_ge(S["x1T_out"], NT - 1)
                pe.wait_ge(S["oT_out"], NT)
                router(NT - 2)
                shared_up(0, 0, early)
                turn_x(NT - 1)
                pe.wait_ge(S["row_sum"], NT)
                shared_up(2, 0, early)
                router(NT - 1)
                shared_up(1, 0, early)
                shared_up(3, 0, early)
                for q in (0, 2, 1, 3):
                    shared_up(q, early, SEQ).then_inc(S["up_made"], 1)
                pe.wait_ge(S["mask_ready"], 1)
                for t in range(NT):
                    for q in range(t):
                        pe.matmul(ps_r[:, 1, t, :], ones, mask[:, q, :], start=(q == 0), stop=False)
                    mm = pe.matmul(ps_r[:, 1, t, :], earlier, mask[:, t, :], start=(t == 0), stop=True)
                for t in range(NT):
                    mm = pe.matmul(ps_c[:, 0:NE], ones, mask[:, t, :], start=(t == 0), stop=(t == NT - 1))
                mm.then_inc(S["pos_made"], 1)
                pe.wait_ge(S["gated"], 2)
                for t in range(NT):
                    if t >= 2:
                        pe.wait_ge(S["acc_ready"], t - 1)
                    for c in range(2):
                        for m in range(2):
                            mm = pe.matmul(dn_bank[t % 2][:, c * 512:(c + 1) * 512], shT[:, m, t * P:(t + 1) * P],
                                           w2[:, m, c * 512:(c + 1) * 512], start=(m == 0), stop=(m == 1))
                    mm.then_inc(S["down_made"], 1)

            @block.scalar
            def _(act):
                def copy_o(t):
                    act.wait_ge(S["oT_made"], t + 1)
                    if t >= 2:
                        act.wait_ge(S["mixed"], t - 1)
                    act.copy(oT[:, t % 2].rearrange("p k c -> p (k c)"), flat_a).then_inc(S["oT_out"], 1)

                def copy_x(t):
                    act.wait_ge(S["x1T_made"], t + 1)
                    act.copy(x1T[:, :, t * P:(t + 1) * P], ps_x[:]).then_inc(S["x1T_out"], 1)

                copy_o(0)
                copy_o(1)
                for t in range(NT):
                    if t + 2 < NT:
                        copy_o(t + 2)
                    if t:
                        copy_x(t - 1)
                        act.wait_ge(S["variance"], t)
                    _norm_squares(act, S, r[:, t % 2, :], st, junk, t)
                    _norm_deviation(act, S, st, t)
                copy_x(NT - 1)
                act.wait_ge(S["logits_made"], NT)
                act.activation(e[:], ps_r[:, 0], ACT.Exp, scale=-1.0).then_inc(S["exps"], 1)
                for m in range(2):
                    act.wait_ge(S["up_made"], 2 * m + 1)
                    act.activation(act_out[:, m, :], up_bank[m], ACT.Silu).then_inc(S["silu_out"], 1)

            @block.vector
            def _(dve):
                steps = 0

                def step(i):
                    nonlocal steps
                    i.then_inc(S["route_step"], 1)
                    steps += 1
                    dve.wait_ge(S["route_step"], steps)

                dve.wait_ge(S["norm_in"], 32)
                for t in range(NT):
                    dve.wait_ge(S["mixed"], t + 1)
                    if t >= 2:
                        dve.wait_ge(S["x1_ready"], t - 1)
                    dve.scalar_tensor_tensor(out=r[:, t % 2, :], in0=x_sb[:, t, :], scalar=ALPHA, in1=ps_mix[:, :],
                                             op0=ALU.mult, op1=ALU.add, accum_out=st[:, 0, t:t + 1]
                                             ).then_inc(S["row_sum"], 1)
                    _norm_mean(dve, S, st, t)
                    _norm_centre(dve, S, r[:, t % 2, :], st, gain, x_sb[:, t, :], t)
                    _norm_variance(dve, S, st, t)
                    _norm_scale(dve, S, st, shift, x_sb[:, t, :], t, S["x1_ready"])
                dve.wait_ge(S["exps"], 1)
                dve.wait_ge(S["small_in"], 32)
                step(dve.tensor_scalar(e[:], e[:], 1.0, None, ALU.add))
                step(dve.reciprocal(s[:], e[:]))
                step(dve.tensor_tensor(sel[:], s[:], rb[:].unsqueeze(1).to_broadcast([P, NT, NE]), ALU.add))
                for t in range(NT):
                    step(dve.max(top8[:, t, :], sel[:, t, :]))
                    step(dve.match_replace(left[:, t, :], top8[:, t, :], sel[:, t, :], NEG))
                dve.tensor_scalar(mask[:], left[:], NEG / 10, None, ALU.is_lt).then_inc(S["mask_ready"], 1)
                dve.wait_ge(S["mask_ready"], 1)
                step(dve.tensor_tensor(gate[:], s[:], mask[:], ALU.mult))
                step(dve.tensor_reduce(gsum[:, 0, :], gate[:], AX.X, ALU.add))
                step(dve.reciprocal(gsum[:, 1, :], gsum[:, 0, :]))
                step(dve.tensor_scalar(gsum[:, 0, :], gsum[:, 1, :], ROUTED_SCALE, None, ALU.mult))
                step(dve.tensor_tensor(gate[:], gate[:], gsum[:, 0, :].unsqueeze(2).to_broadcast([P, NT, NE]), ALU.mult))
                for q in range(3):
                    step(dve.tensor_copy(sb["parts"][:, q, :, :, 1], gate[:]))
                    if q < 2:
                        step(dve.tensor_tensor(gate[:], gate[:], sb["parts"][:, q, :, :, 1], ALU.subtract))
                dve.memset(sb["parts"][:, 2, :, :, 0], 0.0).then_inc(S["tables"], 1)
                for m in range(2):
                    dve.wait_ge(S["silu_out"], m + 1)
                    dve.wait_ge(S["up_made"], 2 * m + 2)
                    dve.tensor_tensor(shT[:, m, :], up_bank[m + 2], act_out[:, m, :], ALU.mult).then_inc(S["gated"], 1)
                dve.wait_ge(S["pos_made"], 1)
                posm = sb["posm"][:, :, 0:NE]
                step(dve.scalar_tensor_tensor(out=posm, in0=ps_r[:, 1], scalar=NOT_ROUTED, in1=mask[:],
                                              op0=ALU.add, op1=ALU.mult))
                step(dve.tensor_scalar(posm, posm, NOT_ROUTED, None, ALU.subtract))
                placed = sb["placed"]
                for t in range(NT):
                    step(dve.tensor_scalar(placed[:, t, :], posm[:, t, :], -1.0,
                                           sb["row"][:, ROPE // 2 + 1 + t:ROPE // 2 + 2 + t], ALU.mult, ALU.add))
                _place_parts(dve, step, sb)
                step(dve.tensor_reduce(cnt[:, 0:1], ps_c[:, 0:NE], AX.X, ALU.max))
                step(dve.tensor_scalar(cnt[:, 1:2], cnt[:, 0:1], float(CAP), 1.0, ALU.is_gt, ALU.add))
                for q in range(2, MAX_PASSES):
                    step(dve.scalar_tensor_tensor(out=cnt[:, q:q + 1], in0=cnt[:, 0:1], scalar=float(q * CAP),
                                                  in1=cnt[:, q - 1:q], op0=ALU.is_gt, op1=ALU.add))
                step(dve.tensor_copy(sb["passes"][:], cnt[:, MAX_PASSES - 1:MAX_PASSES]))
                for t in range(NT):
                    dve.wait_ge(S["down_made"], t + 1)
                    if t >= 2:
                        dve.wait_ge(S[f"acc{t % 2}_out"], 16 * (t // 2))
                    dve.scalar_tensor_tensor(out=acc[:, t % 2, :], in0=x_sb[:, t, :], scalar=ALPHA, in1=dn_bank[t % 2],
                                             op0=ALU.mult, op1=ALU.add).then_inc(S["acc_ready"], 1)
        _restart(nc, S)


SLOTS = 4


class Turn:

    def __init__(self, lap, slot):
        self.lap, self.slot = lap, slot
        self.n = lap * SLOTS + slot
        self.known = isinstance(lap, int)

    def __add__(self, k):
        s = self.slot + k
        return Turn(self.lap + s // SLOTS, s % SLOTS)

    def has(self, k):
        return not self.known or 0 <= self.n + k < NE


def _laps(eng, step):
    for s in range(SLOTS):
        step(Turn(0, s))
    with eng.Fori(1, NE // SLOTS - 1) as lap:
        for s in range(SLOTS):
            step(Turn(lap, s))
    for s in range(SLOTS):
        step(Turn(NE // SLOTS - 1, s))


def _expert_weights(d):
    up = [d[name].rearrange("l e (p k) f -> (l e) p k f", k=KD) for name in ("exp_w1", "exp_w3")]
    return up, d["exp_w2"].rearrange("l e (p j) c -> (l e) p j c", j=2)


def _load_ahead(sp, d, sb, l, landed):
    up, down = _expert_weights(d)
    sp.dma_start(sb["w2_first"][:], down[bass.ds(l * NE, 1)].rearrange("o p j c -> p (o j) c")).then_inc(landed, 16)
    for j in range(2):
        sp.dma_start(sb["w13"][:, 0, j], up[j][bass.ds(l * NE, 1)].rearrange("o p k f -> p (o k) f")).then_inc(landed, 16)


AHEAD = 3 * 16


def _experts(nc, d, sb, l):
    with ExitStack() as ctx:
        S = _named(ctx, nc, "up0_in up1_in dn0_in dn1_in dn2_in dn3_in hot_ready picked_made index_ready "
                            "rows0_in rows1_in rows_turned rows_hi_a rows_hi_b rows_lo up_hi_a up_lo_a up_hi_b up_lo_b dn_hi dn_lo "
                            "half_made up_made silu_out hidden_ready hidden_turned "
                            "hidden_hi hidden_lo down_made y_a y_b added shifted dma_turns ahead_in")
        T = lambda name, shape, dt=F32: ctx.enter_context(nc.sbuf_tensor(name, shape, dt))
        w13 = sb["w13"]
        w2_other = T("w2", [P, SLOTS - 1, 2, D])
        w2 = [sb["w2_first"][:]] + [w2_other[:, i] for i in range(SLOTS - 1)]
        w13_hi = T("w13_hi", [P, 2, KD, FF], F32R)
        w2_hi = T("w2_hi", [P, 2, 2, D], F32R)
        w13_lo = T("w13_lo", [P, 2, KD, FF], F32R)
        w2_lo = T("w2_lo", [P, 2, 2, D], F32R)
        hot = T("hot", [P, 2, NT, CAP], BF16)
        index = T("index", [P, SLOTS], I32)
        y_index = T("y_index", [P, SLOTS], I32)
        gate = T("gate", [P, SLOTS])
        rows = T("rows", [P, 2, D])
        silu, hidden = T("silu", [P, 2, FF]), T("hidden", [P, 2, FF])
        rowsT_hi, rowsT_lo = T("rowsT_hi", [P, 2, KD, CAP], F32R), T("rowsT_lo", [P, 2, KD, CAP], F32R)
        hiddenT_hi, hiddenT_lo = T("hiddenT_hi", [P, 2, 2, CAP], F32R), T("hiddenT_lo", [P, 2, 2, CAP], F32R)
        y = T("y", [P, SLOTS, D])
        ps = lambda name, shape: ctx.enter_context(nc.psum_tensor(name, shape, F32))
        ps_up = [ps(f"ps_up{i}", [P, 2, FF]) for i in range(2)]
        ps_t, ps_y = ps("ps_t", [P, KD, P]), ps("ps_y", [P, D])
        ps_h, ps_p = ps("ps_h", [P, 4, P]), ps("ps_p", [P, 512])
        ident = sb["square"][:, 0:P]
        ident_cap = sb["square"][0:CAP, 0:CAP]
        number = sb["number"][:]
        pad_row = sb["row"][0:CAP, ROPE // 2:ROPE // 2 + 1]
        posm = sb["posm"]
        HALF = KD // 2

        with nc.Block() as block:
            @block.sync
            def _(sp):
                (w1, w3), w2d = _expert_weights(d)
                sp.wait_ge(S["dma_turns"], 2)

                def load(x):
                    e = bass.ds(l * NE + x.n, 1)
                    b = x.slot % 2
                    if x.has(-2):
                        sp.wait_ge(S["up_lo_b"], x.n - 1)
                    if x.has(-1):
                        sp.dma_start(w13[:, b, 0], w1[e].rearrange("o p k f -> p (o k) f")).then_inc(S[f"up{b}_in"], 16)
                        sp.dma_start(w13[:, b, 1], w3[e].rearrange("o p k f -> p (o k) f")).then_inc(S[f"up{b}_in"], 16)
                    if x.has(-SLOTS):
                        sp.wait_ge(S["dn_lo"], x.n - SLOTS + 1)
                    if x.has(-1):
                        sp.dma_start(w2[x.slot], w2d[e].rearrange("o p j c -> p (o j) c")).then_inc(S[f"dn{x.slot}_in"], 16)

                _laps(sp, load)
                sp.wait_ge(S["rows1_in"], 16 * (NE // 2))
                sp.wait_ge(S["up_lo_b"], NE - 1)
                sp.wait_ge(S["dn_lo"], NE - SLOTS + 1)
                _load_ahead(sp, d, sb, l, S["ahead_in"])
                sp.wait_ge(S["ahead_in"], AHEAD)

            @block.gpsimd
            def _(pool):
                def gather(x):
                    b = x.slot % 2
                    pool.wait_ge(S["index_ready"], x.n + 1)
                    if x.has(-2):
                        pool.wait_ge(S["rows_turned"], x.n - 1)
                    pool.sem_inc(S["dma_turns"], 1)
                    pool.indirect_dma_start(rows[0:CAP, b, :], None, d["x1_rows"],
                                            bass.IndirectOffsetOnAxis(ap=index[0:CAP, x.slot:x.slot + 1], axis=0)
                                            ).then_inc(S[f"rows{b}_in"], 16)

                def add(x):
                    pool.wait_ge(S["y_a"], x.n + 1)
                    pool.wait_ge(S["y_b"], x.n + 1)
                    if x.has(-1):
                        pool.wait_ge(S["added"], 16 * x.n)
                    pool.sem_inc(S["dma_turns"], 1)
                    pool.indirect_dma_start(d["acc_rows"], bass.IndirectOffsetOnAxis(ap=y_index[0:CAP, x.slot:x.slot + 1], axis=0),
                                            y[0:CAP, x.slot, :], None, compute_op=ALU.add).then_inc(S["added"], 16)

                gather(Turn(0, 0))
                gather(Turn(0, 1))

                def step(x):
                    if x.has(-2):
                        add(x + -2)
                    if x.has(2):
                        gather(x + 2)
                _laps(pool, step)
                add(Turn(NE // SLOTS - 1, SLOTS - 2))
                add(Turn(NE // SLOTS - 1, SLOTS - 1))
                pool.wait_ge(S["added"], 16 * NE)

            @block.tensor
            def _(pe):
                def pick(x):
                    b = x.slot % 2
                    pe.wait_ge(S["hot_ready"], x.n + 1)
                    if x.has(-1):
                        pe.wait_ge(S["index_ready"], x.n)
                    for t in range(NT):
                        for q in range(3):
                            mm = pe.matmul(ps_p[0:CAP, 0:2], hot[:, b, t, :],
                                           sb["parts"][:, q, t, bass.ds(x.n, 1), :].rearrange("p o v -> p (o v)"),
                                           start=(t == 0 and q == 0), stop=(t == NT - 1 and q == 2))
                    mm.then_inc(S["picked_made"], 1)

                def turn_rows(x):
                    b = x.slot % 2
                    pe.wait_ge(S[f"rows{b}_in"], 16 * (x.lap * (SLOTS // 2) + x.slot // 2 + 1))
                    if x.has(-1):
                        pe.wait_ge(S["rows_lo"], x.n)
                    for k in range(KD):
                        mm = pe.transpose(ps_t[:, k, 0:CAP], rows[0:CAP, b, k::KD], ident_cap)
                    mm.then_inc(S["rows_turned"], 1)

                def up(x, part):
                    b = x.slot % 2
                    if part == 0:
                        pe.wait_ge(S["up_lo_a"], x.n + 1)
                        pe.wait_ge(S["rows_lo"], x.n + 1)
                        if x.has(-2):
                            pe.wait_ge(S["hidden_ready"], x.n - 1)
                    else:
                        pe.wait_ge(S["up_lo_b"], x.n + 1)
                    for k in range(HALF * part, HALF * part + HALF):
                        hi, lo = rowsT_hi[:, b, k, :], rowsT_lo[:, b, k, :]
                        w_hi, w_lo = w13_hi[:, :, k, :], w13_lo[:, :, k, :]
                        pe.matmul(ps_up[b][0:CAP], hi, w_hi, start=(k == 0), stop=False)
                        pe.matmul(ps_up[b][0:CAP], hi, w_lo, start=False, stop=False)
                        mm = pe.matmul(ps_up[b][0:CAP], lo, w_hi, start=False, stop=(k == KD - 1))
                    mm.then_inc(S["up_made" if part else "half_made"], 1)

                def turn_hidden(x):
                    b = x.slot % 2
                    pe.wait_ge(S["hidden_ready"], x.n + 1)
                    if x.has(-1):
                        pe.wait_ge(S["hidden_lo"], x.n)
                    for j in range(2):
                        mm = pe.transpose(ps_h[:, j, 0:CAP], hidden[0:CAP, b, j::2], ident_cap)
                    mm.then_inc(S["hidden_turned"], 1)

                def down(x):
                    b = x.slot % 2
                    pe.wait_ge(S["dn_lo"], x.n + 1)
                    pe.wait_ge(S["hidden_lo"], x.n + 1)
                    if x.has(-1):
                        pe.wait_ge(S["y_a"], x.n)
                        pe.wait_ge(S["y_b"], x.n)
                    for c in range(2):
                        for j in range(2):
                            y_out, cols = ps_y[0:CAP, c * 512:(c + 1) * 512], slice(c * 512, (c + 1) * 512)
                            hi, lo = hiddenT_hi[:, b, j, :], hiddenT_lo[:, b, j, :]
                            w_hi, w_lo = w2_hi[:, b, j, cols], w2_lo[:, b, j, cols]
                            pe.matmul(y_out, hi, w_hi, start=(j == 0), stop=False)
                            pe.matmul(y_out, hi, w_lo, start=False, stop=False)
                            mm = pe.matmul(y_out, lo, w_hi, start=False, stop=(j == 1))
                    mm.then_inc(S["down_made"], 1)

                pick(Turn(0, 0))
                pick(Turn(0, 1))
                turn_rows(Turn(0, 0))

                def step(x):
                    if x.has(2):
                        pick(x + 2)
                    up(x, 0)
                    if x.has(-1):
                        turn_hidden(x + -1)
                    up(x, 1)
                    if x.has(1):
                        turn_rows(x + 1)
                    if x.has(-1):
                        down(x + -1)
                _laps(pe, step)
                last = Turn(NE // SLOTS - 1, SLOTS - 1)
                turn_hidden(last)
                down(last)

            @block.vector
            def _(dve):
                def hots(x):
                    b = x.slot % 2
                    if x.has(-2):
                        dve.wait_ge(S["picked_made"], x.n - 1)
                    for t in range(NT):
                        o = dve.tensor_scalar(hot[:, b, t, :], number, posm[:, t, bass.ds(x.n, 1)], None, ALU.is_equal)
                    o.then_inc(S["hot_ready"], 1)

                def indices(x):
                    b = x.slot % 2
                    dve.wait_ge(S["picked_made"], x.n + 1)
                    if x.has(-SLOTS):
                        dve.wait_ge(S["rows_turned"], x.n - SLOTS + 1)
                        dve.wait_ge(S["y_a"], x.n - SLOTS + 1)
                        dve.wait_ge(S["y_b"], x.n - SLOTS + 1)
                    dve.tensor_copy(gate[0:CAP, x.slot:x.slot + 1], ps_p[0:CAP, 1:2])
                    dve.tensor_scalar(index[0:CAP, x.slot:x.slot + 1], ps_p[0:CAP, 0:1], pad_row, None, ALU.add
                                      ).then_inc(S["index_ready"], 1)

                def hide(x):
                    b = x.slot % 2
                    dve.wait_ge(S["silu_out"], x.n + 1)
                    if x.has(-2):
                        dve.wait_ge(S["hidden_turned"], x.n - 1)
                    dve.tensor_tensor(hidden[0:CAP, b, :], ps_up[b][0:CAP, 1, :], silu[0:CAP, b, :], ALU.mult
                                      ).then_inc(S["hidden_ready"], 1)

                def up_lo(x, half):
                    k = slice(HALF * half, HALF * half + HALF)
                    dve.wait_ge(S["up_hi_b" if half else "up_hi_a"], x.n + 1)
                    dve.tensor_tensor(w13_lo[:, :, k, :], w13[:, x.slot % 2, :, k, :], w13_hi[:, :, k, :].bitcast(F32),
                                      ALU.subtract).then_inc(S["up_lo_b" if half else "up_lo_a"], 1)

                def dn_lo(x):
                    dve.wait_ge(S["dn_hi"], x.n + 1)
                    dve.tensor_tensor(w2_lo[:, x.slot % 2], w2[x.slot], w2_hi[:, x.slot % 2].bitcast(F32), ALU.subtract
                                      ).then_inc(S["dn_lo"], 1)

                def rows_lo(x):
                    b = x.slot % 2
                    for half, k in enumerate((slice(0, HALF), slice(HALF, KD))):
                        dve.wait_ge(S["rows_hi_b" if half else "rows_hi_a"], x.n + 1)
                        o = dve.tensor_tensor(rowsT_lo[:, b, k, :], ps_t[:, k, 0:CAP], rowsT_hi[:, b, k, :].bitcast(F32),
                                              ALU.subtract)
                    o.then_inc(S["rows_lo"], 1)

                def hidden_lo(x):
                    b = x.slot % 2
                    dve.wait_ge(S["hidden_hi"], x.n + 1)
                    dve.tensor_tensor(hiddenT_lo[:, b], ps_h[:, 0:2, 0:CAP], hiddenT_hi[:, b].bitcast(F32), ALU.subtract
                                      ).then_inc(S["hidden_lo"], 1)

                def y_first(x):
                    dve.wait_ge(S["down_made"], x.n + 1)
                    dve.wait_ge(S["index_ready"], x.n + 1)
                    if x.has(-SLOTS):
                        dve.wait_ge(S["added"], 16 * (x.n - SLOTS + 1))
                    dve.tensor_scalar(y[0:CAP, x.slot, 0:512], ps_y[0:CAP, 0:512], gate[0:CAP, x.slot:x.slot + 1], None,
                                      ALU.mult)
                    dve.tensor_copy(y_index[0:CAP, x.slot:x.slot + 1], index[0:CAP, x.slot:x.slot + 1]).then_inc(S["y_a"], 1)

                hots(Turn(0, 0))
                hots(Turn(0, 1))
                indices(Turn(0, 0))
                indices(Turn(0, 1))
                hots(Turn(0, 2))
                up_lo(Turn(0, 0), 0)
                up_lo(Turn(0, 0), 1)
                rows_lo(Turn(0, 0))

                def step(x):
                    if x.has(3):
                        hots(x + 3)
                    if x.has(2):
                        indices(x + 2)
                    if x.has(-1):
                        hidden_lo(x + -1)
                    if x.has(1):
                        up_lo(x + 1, 0)
                    hide(x)
                    if x.has(1):
                        rows_lo(x + 1)
                        up_lo(x + 1, 1)
                    dn_lo(x)
                    if x.has(-1):
                        y_first(x + -1)
                _laps(dve, step)
                last = Turn(NE // SLOTS - 1, SLOTS - 1)
                hidden_lo(last)
                y_first(last)
                dve.wait_ge(S["hot_ready"], NE)
                dve.wait_ge(S["picked_made"], NE)
                shifts = 0

                def step(i):
                    nonlocal shifts
                    i.then_inc(S["shifted"], 1)
                    shifts += 1
                    dve.wait_ge(S["shifted"], shifts)

                step(dve.tensor_scalar(posm[:], posm[:], float(CAP), None, ALU.subtract))
                step(dve.tensor_scalar(sb["placed"][:], sb["placed"][:], float(CAP), None, ALU.add))
                _place_parts(dve, step, sb)

            @block.scalar
            def _(act):
                def up_hi(x, half):
                    k = slice(HALF * half, HALF * half + HALF)
                    if not half and x.has(-1):
                        act.wait_ge(S[f"up{x.slot % 2}_in"], 32 * (x.lap * (SLOTS // 2) + x.slot // 2 + x.slot % 2))
                    if x.has(-1):
                        act.wait_ge(S["up_made" if half else "half_made"], x.n)
                    act.copy(w13_hi[:, :, k, :], w13[:, x.slot % 2, :, k, :]).then_inc(S["up_hi_b" if half else "up_hi_a"], 1)

                def dn_hi(x):
                    if x.has(-1):
                        act.wait_ge(S[f"dn{x.slot}_in"], 16 * (x.lap + 1 if x.slot else x.lap))
                    if x.has(-2):
                        act.wait_ge(S["down_made"], x.n - 1)
                    act.copy(w2_hi[:, x.slot % 2], w2[x.slot]).then_inc(S["dn_hi"], 1)

                def rows_hi(x):
                    b = x.slot % 2
                    act.wait_ge(S["rows_turned"], x.n + 1)
                    if x.has(-2):
                        act.wait_ge(S["up_made"], x.n - 1)
                    act.copy(rowsT_hi[:, b, 0:HALF, :], ps_t[:, 0:HALF, 0:CAP]).then_inc(S["rows_hi_a"], 1)
                    act.copy(rowsT_hi[:, b, HALF:KD, :], ps_t[:, HALF:KD, 0:CAP]).then_inc(S["rows_hi_b"], 1)

                def hidden_hi(x):
                    act.wait_ge(S["hidden_turned"], x.n + 1)
                    if x.has(-2):
                        act.wait_ge(S["down_made"], x.n - 1)
                    act.copy(hiddenT_hi[:, x.slot % 2], ps_h[:, 0:2, 0:CAP]).then_inc(S["hidden_hi"], 1)

                def gates(x):
                    act.wait_ge(S["up_made"], x.n + 1)
                    if x.has(-2):
                        act.wait_ge(S["hidden_ready"], x.n - 1)
                    act.activation(silu[0:CAP, x.slot % 2, :], ps_up[x.slot % 2][0:CAP, 0, :], ACT.Silu).then_inc(S["silu_out"], 1)

                def y_second(x):
                    act.wait_ge(S["down_made"], x.n + 1)
                    act.wait_ge(S["index_ready"], x.n + 1)
                    if x.has(-SLOTS):
                        act.wait_ge(S["added"], 16 * (x.n - SLOTS + 1))
                    act.activation(y[0:CAP, x.slot, 512:D], ps_y[0:CAP, 512:D], ACT.Copy, scale=gate[0:CAP, x.slot:x.slot + 1]
                                   ).then_inc(S["y_b"], 1)

                up_hi(Turn(0, 0), 0)
                up_hi(Turn(0, 0), 1)
                rows_hi(Turn(0, 0))

                def step(x):
                    if x.has(1):
                        up_hi(x + 1, 0)
                    if x.has(-1):
                        hidden_hi(x + -1)
                    gates(x)
                    if x.has(1):
                        rows_hi(x + 1)
                        up_hi(x + 1, 1)
                    dn_hi(x)
                    if x.has(-1):
                        y_second(x + -1)
                _laps(act, step)
                last = Turn(NE // SLOTS - 1, SLOTS - 1)
                hidden_hi(last)
                y_second(last)
        _restart(nc, S)


def _second_norm(nc, d, sb, l):
    with ExitStack() as ctx:
        S = _named(ctx, nc, NORM_SEMS + " gain2_in shift2_in acc0_in acc1_in acc2_in acc3_in x_ready")
        acc = ctx.enter_context(nc.sbuf_tensor("acc5", [P, NT, D], F32))
        junk = ctx.enter_context(nc.sbuf_tensor("junk5", [P, D], F32))
        sums = ctx.enter_context(nc.sbuf_tensor("sums5", [P, 2, D], F32))
        st = ctx.enter_context(nc.sbuf_tensor("st5", [P, 5, NT], F32))
        gain = ctx.enter_context(nc.sbuf_tensor("gain2", [P, D], F32))
        shift = ctx.enter_context(nc.sbuf_tensor("shift2", [P, D], F32))
        with nc.Block() as block:
            @block.sync
            def _(sp):
                for t in range(NT):
                    sp.dma_start(acc[:, t, :], d["acc_rows"][t * P:(t + 1) * P, :]).then_inc(S[f"acc{t}_in"], 16)
                    if t < 2:
                        tile, name = ((gain, "ln2_g"), (shift, "ln2_b"))[t]
                        sp.dma_start(tile[:], d[name][bass.ds(l, 1)].to_broadcast([P, D])).then_inc(S[("gain2_in", "shift2_in")[t]], 16)

            @block.scalar
            def _(act):
                def row_sum(t):
                    act.wait_ge(S[f"acc{t}_in"], 16)
                    if t >= 2:
                        act.wait_ge(S["row_sum"], t - 1)
                    act.activation(sums[:, t % 2, :], acc[:, t, :], ACT.Copy, accum_out=st[:, 0, t:t + 1]).then_inc(S["row_sum"], 1)

                row_sum(0)
                for t in range(NT):
                    if t:
                        act.wait_ge(S["variance"], t)
                    _norm_squares(act, S, acc[:, t, :], st, junk, t)
                    if t + 1 < NT:
                        row_sum(t + 1)
                    _norm_deviation(act, S, st, t)

            @block.vector
            def _(dve):
                x = sb["x"]
                for t in range(NT + 1):
                    if t < NT:
                        _norm_mean(dve, S, st, t)
                        if t == 0:
                            dve.wait_ge(S["gain2_in"], 16)
                        _norm_centre(dve, S, acc[:, t, :], st, gain, x[:, t, :], t)
                    if t == 1:
                        dve.wait_ge(S["shift2_in"], 16)
                    if t:
                        _norm_scale(dve, S, st, shift, x[:, t - 1, :], t - 1, S["x_ready"])
                    if t < NT:
                        _norm_variance(dve, S, st, t)
        _restart(nc, S)


def trunk(nc, d, out):
    with ExitStack() as ctx:
        T = lambda name, shape, dt=F32: ctx.enter_context(nc.sbuf_tensor(name, shape, dt))
        d["x1_rows"] = nc.dram_tensor("x1_rows", [ACC_ROWS, D], F32).ap()
        d["acc_rows"] = nc.dram_tensor("acc_rows", [ACC_ROWS, D], F32).ap()
        d["bias_rows"] = nc.dram_tensor("bias_rows", [10, SPAN + 1], F32).ap()
        d["bias_tiles"] = nc.dram_tensor("bias_tiles", [P, 10, SEQ], F32).ap()
        sb = {"x": T("x_sb", [P, NT, D]),
              "mask": T("mask", [P, SEQ]), "square": T("square", [P, 3 * P]),
              "row": T("row", [P, ROPE // 2 + 1 + NT]), "rope": T("rope", [P, NT, 2, ROPE // 2]),
              "number": T("number", [P, CAP], BF16), "passes": T("passes", [P, 1], I32)}
        out_stored = ctx.enter_context(nc.semaphore("out_stored"))
        _setup(nc, d, sb)
        with nc.Fori(0, DEPTH) as l:
            with ExitStack() as routed:
                with ExitStack() as late:
                    right = lambda stack, name, shape, dt=F32: stack.enter_context(nc.sbuf_tensor(name, shape, dt, side="right"))
                    with ExitStack() as mixer:
                        M = lambda name, shape: mixer.enter_context(nc.sbuf_tensor(name, shape, F32))
                        sb |= {"dqkT": M("dqkT", [P, 6, SEQ]), "sqkT": M("sqkT", [P, 4, SEQ]),
                               "dv": M("dv", [P, NT, H_DIL * HD]), "sv": M("sv", [P, NT, H_DSA * HD]),
                               "mqT": M("mqT", [P, H_MLA, SEQ]), "mkT": M("mkT", [P, H_MLA, SEQ]),
                               "mv": M("mv", [P, NT, H_MLA * HD]), "pen": M("pen", [P, PEN_COLUMNS])}
                        _projections(nc, d, sb, l)
                        sb |= {"posm": right(routed, "posm", [P, NT, NE]), "placed": right(routed, "placed", [P, NT, NE]),
                               "parts": right(routed, "parts", [P, 3, NT, NE, 2], BF16)}
                        sb |= {"o": right(late, "o_sb", [P, NT, D]), "w_out": right(late, "w_out_sb", [P, KD, D])}
                        _attention(nc, d, sb, l)
                    left = lambda name, shape: routed.enter_context(nc.sbuf_tensor(name, shape, F32))
                    sb |= {"w13": left("w13", [P, 2, 2, KD, FF]), "w2_first": left("w2_first", [P, 2, D])}
                    _mix_and_route(nc, d, sb, l)
                passes = nc.values_load(sb["passes"][0:1, 0:1], min_val=1, max_val=MAX_PASSES)
                with nc.Fori(0, passes) as _:
                    _experts(nc, d, sb, l)
            _second_norm(nc, d, sb, l)
        with nc.Block() as block:
            @block.sync
            def _(sp):
                sp.dma_start(out.rearrange("o (t p) m -> p (o t) m", p=P), sb["x"][:]).then_inc(out_stored, 16)
                sp.wait_ge(out_stored, 16)


_INS = ["x", "positions", "w_in", "mla_q_norm", "mla_w_uq", "mla_kv_norm", "mla_w_ukv", "w_out", "ln1_g", "ln1_b",
        "router_w", "router_bias", "exp_w1", "exp_w3", "exp_w2", "sh_w1", "sh_w3", "sh_w2", "ln2_g", "ln2_b", "rel_bias"]


def kernel(**inputs):
    import concourse.bacc as _bacc
    from concourse.bass_utils import run_bass_kernel_spmd as _run

    nc = _bacc.Bacc("TRN2", target_bir_lowering=False, num_devices=1)
    arrays = {n: np.ascontiguousarray(inputs[n]) for n in _INS}
    arrays.update(_constants())
    d = {n: nc.dram_tensor(n, a.shape, mybir.dt.from_np(a.dtype), kind="ExternalInput").ap() for n, a in arrays.items()}
    out = nc.dram_tensor("out", [1, SEQ, D], F32, kind="ExternalOutput").ap()
    trunk(nc, d, out)
    r = _run(nc, [arrays], core_ids=[0])
    return r.results[0]["out"]
```
